# Optimizing a Trainium2 kernel written in Bass

```python
import jax, jax.numpy as jnp
from jax import lax
import numpy as np

D_MODEL = 1024
BATCH = 1
SEQ = 2048
DEPTH = 1
DEC_BATCH = 8
DEC_SEQ = 1
PAST_LEN = 2048
PAGE_SIZE = 128

N_META = 16
WINDOW = 128
HEAD_DIM = 64
ATT_WIDTH = D_MODEL // 2
ATT_HEADS = ATT_WIDTH // HEAD_DIM
KV_HEADS = ATT_HEADS // 4
GQA_GROUP = ATT_HEADS // KV_HEADS
HG_WIDTH = D_MODEL - ATT_WIDTH
HG_EXPAND = 128
HG_HEADS = HG_WIDTH // HG_EXPAND
HG_KDIM = HG_EXPAND
HG_VDIM = HG_WIDTH // HG_HEADS
HG_CHUNK = 64
MIX_WIDTH = ATT_WIDTH + HG_WIDTH
PROJ_WIDTH = 2 * ATT_WIDTH + 2 * KV_HEADS * HEAD_DIM + 2 * HG_HEADS * HG_KDIM + 2 * HG_WIDTH
EPS = 1e-6
NEG_BIG = -1e30
TINY = 1e-30

kernel_name = "hymba_swa_sink_hgrn2_decode_step"

def rms_norm(x, w):
    x32 = x.astype(jnp.float32)
    y = x32 * lax.rsqrt(jnp.mean(x32 * x32, axis=-1, keepdims=True) + EPS) * w.astype(jnp.float32)
    return y.astype(x.dtype)

def project(x, norm_w, w_in, q_norm_w, k_norm_w, lb):
    lead = x.shape[:-1]
    p = rms_norm(x, norm_w) @ w_in
    sizes = [ATT_WIDTH, KV_HEADS * HEAD_DIM, KV_HEADS * HEAD_DIM, ATT_WIDTH,
             HG_HEADS * HG_KDIM, HG_HEADS * HG_KDIM, HG_WIDTH, HG_WIDTH]
    qa, ka, va, ga, qh, fh, ih, gh = jnp.split(p, np.cumsum(sizes)[:-1].tolist(), axis=-1)
    qa = rms_norm(qa.reshape(*lead, KV_HEADS, GQA_GROUP, HEAD_DIM), q_norm_w)
    ka = rms_norm(ka.reshape(*lead, KV_HEADS, HEAD_DIM), k_norm_w)
    va = va.reshape(*lead, KV_HEADS, HEAD_DIM)
    hq = jax.nn.silu(qh.astype(jnp.float32)).reshape(*lead, HG_HEADS, HG_KDIM)
    z = fh.astype(jnp.float32).reshape(*lead, HG_HEADS, HG_KDIM)
    hk = (1.0 - lb) * jax.nn.sigmoid(-z)
    f = lb + (1.0 - lb) * jax.nn.sigmoid(z)
    hg = jnp.log(jnp.maximum(f, TINY))
    hv = ih.astype(jnp.float32).reshape(*lead, HG_HEADS, HG_VDIM)
    return qa, ka, va, ga, hq, hk, hv, hg, gh

def window_mask(qpos, kpos):
    qq = qpos[..., :, None]
    meta = jnp.arange(N_META) <= qq
    kk = kpos[..., None, :]
    band = (kk >= N_META) & (kk <= qq) & (qq - kk < WINDOW)
    return jnp.concatenate([meta, band], axis=-1)

def sink_attention(q, k, v, mask, sink):
    s = jnp.einsum('bnqhgd,bnchd->bnhgqc', q, k).astype(jnp.float32) * (HEAD_DIM ** -0.5)
    s = jnp.where(mask[None, :, None, None], s, NEG_BIG)
    sink_col = jnp.broadcast_to(sink.astype(jnp.float32).reshape(1, 1, KV_HEADS, GQA_GROUP, 1, 1), s.shape[:-1] + (1,))
    prob = jax.nn.softmax(jnp.concatenate([s, sink_col], axis=-1), axis=-1)[..., :-1]
    return jnp.einsum('bnhgqc,bnchd->bnqhgd', prob.astype(v.dtype), v)

def window_attention_prompt(q, k, v, sink):
    B, L = q.shape[:2]
    nb = -(-L // WINDOW)
    pad = nb * WINDOW - L
    padf = lambda a: jnp.pad(a, [(0, 0), (0, pad)] + [(0, 0)] * (a.ndim - 2))
    qb = padf(q).reshape(B, nb, WINDOW, KV_HEADS, GQA_GROUP, HEAD_DIM)
    kb = padf(k).reshape(B, nb, WINDOW, KV_HEADS, HEAD_DIM)
    vb = padf(v).reshape(B, nb, WINDOW, KV_HEADS, HEAD_DIM)
    band = lambda a: jnp.concatenate([jnp.pad(a, [(0, 0), (1, 0), (0, 0), (0, 0), (0, 0)])[:, :-1], a], axis=2)
    meta = lambda a: jnp.broadcast_to(a[:, None, :N_META], (B, nb, N_META, KV_HEADS, HEAD_DIM))
    keys = jnp.concatenate([meta(k), band(kb)], axis=2)
    vals = jnp.concatenate([meta(v), band(vb)], axis=2)
    blk = jnp.arange(nb)[:, None]
    qpos = blk * WINDOW + jnp.arange(WINDOW)[None]
    kpos = (blk - 1) * WINDOW + jnp.arange(2 * WINDOW)[None]
    o = sink_attention(qb, keys, vals, window_mask(qpos, kpos), sink)
    return o.reshape(B, nb * WINDOW, KV_HEADS, GQA_GROUP, HEAD_DIM)[:, :L]

def window_attention_sample(q, k, v, meta_k, meta_v, buf_k, buf_v, sink):
    T = q.shape[1]
    wb = buf_k.shape[1]
    qpos = PAST_LEN + jnp.arange(T)
    kpos = jnp.concatenate([PAST_LEN - wb + jnp.arange(wb), PAST_LEN + jnp.arange(T)])
    keys = jnp.concatenate([meta_k, buf_k, k], axis=1)[:, None]
    vals = jnp.concatenate([meta_v, buf_v, v], axis=1)[:, None]
    return sink_attention(q[:, None], keys, vals, window_mask(qpos, kpos)[None], sink)[:, 0]

def hgrn_chunk(S0, q, k, v, g):
    C = q.shape[1]
    G = jnp.cumsum(g, axis=1)
    o_inter = jnp.einsum('bthk,bhkv->bthv', q * jnp.exp(G), S0)
    causal = jnp.tril(jnp.ones((C, C), dtype=bool))[None, :, :, None, None]
    diff = G[:, :, None] - G[:, None, :]
    decay = jnp.where(causal, jnp.exp(jnp.where(causal, diff, 0.0)), 0.0)
    A = jnp.einsum('btshk,bthk,bshk->btsh', decay, q, k)
    o = o_inter + jnp.einsum('btsh,bshv->bthv', A, v)
    G_end = G[:, -1]
    S1 = jnp.exp(G_end)[..., None] * S0 + jnp.einsum('bshk,bshv->bhkv', k * jnp.exp(G_end[:, None] - G), v)
    return S1, o

def hgrn_prompt(q, k, v, g):
    B = q.shape[0]
    S0 = jnp.zeros((B, HG_HEADS, HG_KDIM, HG_VDIM), jnp.float32)
    S, o_meta = hgrn_chunk(S0, q[:, :N_META], k[:, :N_META], v[:, :N_META], g[:, :N_META])
    nc = (q.shape[1] - N_META) // HG_CHUNK
    to_chunks = lambda a: jnp.moveaxis(a[:, N_META:].reshape(B, nc, HG_CHUNK, *a.shape[2:]), 1, 0)
    S, o_real = lax.scan(lambda s, xs: hgrn_chunk(s, *xs), S, (to_chunks(q), to_chunks(k), to_chunks(v), to_chunks(g)))
    o_real = jnp.moveaxis(o_real, 0, 1).reshape(B, nc * HG_CHUNK, HG_HEADS, HG_VDIM)
    return jnp.concatenate([o_meta, o_real], axis=1), S

def merge(att_o, ga, hg_o, gh, hg_norm_w, w_out):
    lead = ga.shape[:-1]
    att = att_o.reshape(*lead, ATT_WIDTH) * jax.nn.silu(ga)
    hg = rms_norm(hg_o, hg_norm_w).reshape(*lead, HG_WIDTH).astype(gh.dtype) * jax.nn.silu(gh)
    return jnp.concatenate([att, hg], axis=-1) @ w_out

def setup_inputs(seed: int = 0) -> dict:
    key = jax.random.key(seed)
    ks = jax.random.split(key, 18)
    nrm = jax.random.normal
    w_buf = min(WINDOW, PAST_LEN)
    return {
        "x_prompt": nrm(ks[0], (BATCH, SEQ, D_MODEL), jnp.float32),
        "x_sample": nrm(ks[1], (DEC_BATCH, DEC_SEQ, D_MODEL), jnp.float32),
        "cache_win_k": nrm(ks[2], (DEC_BATCH, DEPTH, w_buf, KV_HEADS, HEAD_DIM), jnp.float32),
        "cache_win_v": nrm(ks[3], (DEC_BATCH, DEPTH, w_buf, KV_HEADS, HEAD_DIM), jnp.float32),
        "cache_meta_k": nrm(ks[4], (DEC_BATCH, DEPTH, N_META, KV_HEADS, HEAD_DIM), jnp.float32),
        "cache_meta_v": nrm(ks[5], (DEC_BATCH, DEPTH, N_META, KV_HEADS, HEAD_DIM), jnp.float32),
        "state_hgrn": 0.5 * nrm(ks[6], (DEC_BATCH, DEPTH, HG_HEADS, HG_KDIM, HG_VDIM), jnp.float32),
        "meta_tokens": nrm(ks[7], (N_META, D_MODEL), jnp.float32),
        "norm_w": 1.0 + 0.02 * nrm(ks[8], (DEPTH, D_MODEL), jnp.float32),
        "w_in": nrm(ks[9], (DEPTH, D_MODEL, PROJ_WIDTH), jnp.float32) * D_MODEL ** -0.5,
        "q_norm_w": 1.0 + 0.02 * nrm(ks[10], (DEPTH, HEAD_DIM), jnp.float32),
        "k_norm_w": 1.0 + 0.02 * nrm(ks[11], (DEPTH, HEAD_DIM), jnp.float32),
        "attn_sinks": 0.5 * nrm(ks[12], (DEPTH, ATT_HEADS), jnp.float32),
        "hg_lb_logits": 0.1 * nrm(ks[13], (DEPTH, HG_HEADS * HG_KDIM), jnp.float32),
        "hg_norm_w": 1.0 + 0.02 * nrm(ks[14], (DEPTH, HG_VDIM), jnp.float32),
        "w_out": nrm(ks[15], (DEPTH, MIX_WIDTH, D_MODEL), jnp.float32) * MIX_WIDTH ** -0.5,
    }

def reference(x_prompt, x_sample, cache_win_k, cache_win_v, cache_meta_k, cache_meta_v, state_hgrn,
              meta_tokens, norm_w, w_in, q_norm_w, k_norm_w, attn_sinks, hg_lb_logits, hg_norm_w, w_out):
    lb_p = jax.nn.softmax(hg_lb_logits.astype(jnp.float32), axis=0)
    lb_all = (jnp.cumsum(lb_p, axis=0) - lb_p[0]).reshape(DEPTH, HG_HEADS, HG_KDIM)
    B = x_prompt.shape[0]
    w_buf = cache_win_k.shape[2]
    xp = jnp.concatenate([jnp.broadcast_to(meta_tokens[None].astype(x_prompt.dtype), (B, N_META, D_MODEL)), x_prompt], axis=1)
    xs = x_sample
    wkp, wvp, mkp, mvp, hsp, wks, wvs, hss = [], [], [], [], [], [], [], []
    for l in range(DEPTH):
        qa, ka, va, ga, hq, hk, hv, hg, gh = project(xp, norm_w[l], w_in[l], q_norm_w[l], k_norm_w[l], lb_all[l])
        att = window_attention_prompt(qa, ka, va, attn_sinks[l])
        hgo, S_p = hgrn_prompt(hq, hk, hv, hg)
        xp = xp + merge(att, ga, hgo, gh, hg_norm_w[l], w_out[l])
        wkp.append(ka[:, -w_buf:]); wvp.append(va[:, -w_buf:])
        mkp.append(ka[:, :N_META]); mvp.append(va[:, :N_META])
        hsp.append(S_p)
        qa, ka, va, ga, hq, hk, hv, hg, gh = project(xs, norm_w[l], w_in[l], q_norm_w[l], k_norm_w[l], lb_all[l])
        att = window_attention_sample(qa, ka, va, cache_meta_k[:, l], cache_meta_v[:, l], cache_win_k[:, l], cache_win_v[:, l], attn_sinks[l])
        S_s, hgo = hgrn_chunk(state_hgrn[:, l].astype(jnp.float32), hq, hk, hv, hg)
        xs = xs + merge(att, ga, hgo, gh, hg_norm_w[l], w_out[l])
        wks.append(jnp.concatenate([cache_win_k[:, l], ka], axis=1)[:, -w_buf:])
        wvs.append(jnp.concatenate([cache_win_v[:, l], va], axis=1)[:, -w_buf:])
        hss.append(S_s)
    y_prompt = xp[:, N_META:]
    y_sample = xs
    return (y_prompt, y_sample, jnp.stack(wkp, 1), jnp.stack(wvp, 1), jnp.stack(mkp, 1), jnp.stack(mvp, 1), jnp.stack(hsp, 1),
            jnp.stack(wks, 1), jnp.stack(wvs, 1), jnp.stack(hss, 1))


_drawn_inputs = setup_inputs


def setup_inputs(seed=0):
    import zlib

    import numpy as np

    out = dict(_drawn_inputs(seed))
    spreads = {}
    factors = {'cache_meta_k': 4.264,
     'cache_meta_v': 3.905,
     'norm_w': 2.822,
     'q_norm_w': 8.0,
     'k_norm_w': 2.743,
     'attn_sinks': 8.0,
     'hg_norm_w': 7.355}
    for name, (base, spread) in spreads.items():
        noise = np.random.default_rng([zlib.crc32(name.encode()), seed]).standard_normal(out[name].shape)
        drawn = base * np.exp(spread * noise) if base else spread * noise
        out[name] = __import__('jax').numpy.asarray(drawn.astype(out[name].dtype))
    for name, factor in factors.items():
        out[name] = (out[name] * factor).astype(out[name].dtype)
    return out
```

```python
from collections import namedtuple
from contextlib import ExitStack

import numpy as np
import concourse.bass as bass
from concourse import mybir

F32 = mybir.dt.float32
F32R = mybir.dt.float32r
BF16 = mybir.dt.bfloat16
ALU = mybir.AluOpType
ACT = mybir.ActivationFunctionType
AX = mybir.AxisListType

P = 128
D = 1024
KT = D // P
SEQ = 2048
TILES = SEQ // P + 1
META = 16
NS = 8
SROW = 32
HD = 64
AH = 8
KVH = 2
HH = 4
HW = 512
EPS = 1e-6
TINY = 1e-30
PAIRS = [1, 2, 4, 8, 16]
ATT_COLS = 2 * HW + 2 * KVH * HD
KEYS = META + 2 * P
SCALE = HD ** -0.5

Tile = namedtuple("Tile", "n half slot")


def tile(it, c):
    return Tile(2 * it + c, it + c // 2, c % 2)


def wait(eng, sem, count):
    if isinstance(count, int) and count <= 0:
        return
    eng.wait_ge(sem, count)


def rows_of(dram, t):
    return dram[bass.ds((t.n - 1) * P, P), :]


def hgrn_pass(nc, x_prompt, x_sample, meta_tokens, w_in, norm_w, lb_logits, hg_norm_w, state, consts,
              mixed, mixed_sample, new_state, new_state_sample):
    with ExitStack() as ctx:
        def sb(name, shape, dt=F32):
            return ctx.enter_context(nc.sbuf_tensor("h_" + name, shape, dt))

        def bank(name):
            return ctx.enter_context(nc.psum_tensor("h_" + name, [P, 512], F32))

        def sem(name):
            return nc.alloc_semaphore(name="h_" + name)

        w_hi = sb("w_hi", [P, KT, 4 * HW], F32R)
        w_lo = sb("w_lo", [P, KT, 4 * HW], F32R)
        cst = sb("cst", [P, P + 192])
        ident, mask_a, mask_b = cst[:, 0:P], cst[:, P:P + 96], cst[:, P + 96:P + 192]
        nw = sb("nw", [P, KT])
        lbt = sb("lbt", [P, 6, HH])
        lb, oml = lbt[:, 4, :], lbt[:, 5, :]
        hgnw = sb("hgnw", [P, P])
        half_power = sb("half_power", [P, HH])
        X = [sb(f"x{i}", [P, D]) for i in range(2)]
        h_hi = [sb(f"h_hi{i}", [P, KT, P], F32R) for i in range(2)]
        h_lo = [sb(f"h_lo{i}", [P, KT, P], F32R) for i in range(2)]
        ss = sb("ss", [P, 1])
        var = sb("var", [P, 1])
        rstd = sb("rstd", [P, 1])
        junk_x = sb("junk_x", [P, D], BF16)
        junk_o = sb("junk_o", [P, HW], BF16)
        z_nat = sb("z_nat", [P, HW])
        q_nat = sb("q_nat", [P, HW])
        q_sig = sb("q_sig", [P, HW])
        g_sig = q_sig
        G = [sb(f"g{i}", [P, HW]) for i in range(2)]
        V = [sb(f"v{i}", [P, HW]) for i in range(2)]
        F = sb("f", [P, HW])
        Kz = sb("kz", [P, HW])
        Qz = sb("qz", [P, HW])
        LV = sb("lv", [P, 4, HW])
        Q, K = [LV[:, i, :] for i in (0, 1)], [LV[:, i, :] for i in (2, 3)]
        R = [sb(f"r{i}", [P, HW]) for i in range(2)]
        TT = sb("tt", [P, 512])
        TE = [sb(f"te{i}", [P, HH]) for i in range(2)]
        PR = sb("pr", [P, 2, HH, 3, 32])
        A = sb("a", [P, HH, P])
        KN = sb("kn", [P, HW])
        S = sb("s", [P, HW])
        MIX = [sb(f"mix{i}", [P, HW]) for i in range(2)]
        MIX_S = sb("mix_s", [64, HW])
        oss = sb("oss", [P, HH])
        ovar = sb("ovar", [P, HH])
        orstd = sb("orstd", [P, HH])

        bank_a, bank_b, bank_t = bank("bank_a"), bank("bank_b"), bank("bank_t")
        near_a, near_b, far = bank("near_a"), bank("near_b"), bank("far")
        bank_o, bank_s = bank("bank_o"), bank("bank_s")

        c_loaded, nw_loaded, x_zeroed, power_set = sem("c_loaded"), sem("nw_loaded"), sem("x_zeroed"), sem("power_set")
        lb_loaded = sem("lb_loaded")
        lbd, lbe = sem("lbd"), sem("lbe")
        w_loaded = [sem(f"w_loaded{i}") for i in range(KT)]
        w_high, w_ready = sem("w_high"), sem("w_ready")
        x_loaded = [sem(f"x_loaded{i}") for i in range(2)]
        x_squared, var_done, rstd_done, x_scaled = sem("x_squared"), sem("var_done"), sem("rstd_done"), sem("x_scaled")
        xt, h_high, h_low = sem("xt"), sem("h_high"), sem("h_low")
        f_proj, q_proj, i_proj, g_proj = sem("f_proj"), sem("q_proj"), sem("i_proj"), sem("g_proj")
        z_copied, q_sigm, q_silu, v_copied = sem("z_copied"), sem("q_sigm"), sem("q_silu"), sem("v_copied")
        g_sigm, g_silu, g_done = sem("g_sigm"), sem("g_silu"), sem("g_done")
        zt, qt, fk_sig, fk_aff, fk_done, q0_done = sem("zt"), sem("qt"), sem("fk_sig"), sem("fk_aff"), sem("fk_done"), sem("q0_done")
        totals, q_lev, k_lev, lev_mm = sem("totals"), sem("q_lev"), sem("k_lev"), sem("lev_mm")
        near_masked, near_summed, far_copied = sem("near_masked"), sem("near_summed"), sem("far_copied")
        o_mm, k_turned, k_nat, s_mm, s_new = sem("o_mm"), sem("k_turned"), sem("k_nat"), sem("s_mm"), sem("s_new")
        o_squared, ovar_done, orstd_done, mix_done = sem("o_squared"), sem("ovar_done"), sem("orstd_done"), sem("mix_done")
        mix_stored = sem("mix_stored")
        meta_k, qm_zeroed, qm_done = sem("meta_k"), sem("qm_zeroed"), sem("qm_done")
        km_done, outer_mm, s1_done, so_mm = sem("km_done"), sem("outer_mm"), sem("s1_done"), sem("so_mm")
        near_added, rest_stored, a_zeroed = sem("near_added"), sem("rest_stored"), sem("a_zeroed")
        st_loaded = [sem(f"st_loaded{i}") for i in range(4)]
        s1_stored = [sem(f"s1_stored{i}") for i in range(4)]

        FIRST, LAST = 2, TILES - 4
        LOOP = (FIRST // 2, (LAST + 1) // 2)
        ring = [R[0], R[1], MIX[0], MIX[1]]
        w_slots = [LV[:, i, :] for i in range(4)] + [buffer[:, :] for buffer in ring]
        qm = LV
        km = [PR[:, :, :, :, :].rearrange("p a h l c -> p (a h l c)")[:, 0:HW], TT[:, :]]
        outer_bank = [far, near_a]
        sample_rows = slice(SROW, SROW + NS)

        def blocks(ap, b):
            return ap.rearrange("p (n two b) -> p n two b", two=2, b=b)

        def tot(b):
            if b == 1:
                return F[:, :]
            at = 512 - 1024 // b
            return TT[:, at:at + HW // b]

        def half(buffer, a):
            return buffer[:, 4 * a:4 * a + 4, :].rearrange("p k t -> p (k t)")

        def first_tile(t):
            return isinstance(t.n, int) and t.n == 0

        def fi_bank(t):
            return near_a if first_tile(t) else bank_a

        def qg_bank(t):
            return near_b if first_tile(t) else bank_b

        def x_bank(t, a):
            if isinstance(t.n, int) and t.n < 2 and a == 1:
                return (bank_s, bank_o)[t.n]
            return bank_t

        block = ctx.enter_context(nc.Block())

        @block.sync
        def _(sp):
            sp.dma_start(nw[:, :], norm_w).then_inc(nw_loaded, 16)
            sp.wait_ge(x_zeroed, 1)
            sp.dma_start(X[0][0:META, :], meta_tokens).then_inc(x_loaded[0], 16)
            sp.dma_start(X[0][SROW:SROW + NS, :], x_sample).then_inc(x_loaded[0], 16)
            sp.dma_start(cst[:, :], consts).then_inc(c_loaded, 16)

            def load_x(t):
                wait(sp, xt, 2 * t.n - 2)
                sp.dma_start(X[t.slot][:, :], rows_of(x_prompt, t)).then_inc(x_loaded[t.slot], 16)

            def store_mixed(t):
                sp.wait_ge(mix_done, t.n + 1)
                sp.dma_start(mixed[bass.ds((t.n - 1) * P, P), HW:D], MIX[t.slot][:, :]).then_inc(mix_stored, 16)

            def by_key(states):
                return states.rearrange("h k v -> k h v")

            def by_head(buffer):
                return buffer[:, :].rearrange("p (h v) -> p h v", h=HH)

            w_at = [ATT_COLS + HW, ATT_COLS, ATT_COLS + 2 * HW, ATT_COLS + 3 * HW]
            for c in range(4):
                for k in range(KT):
                    j = KT * c + k
                    wait(sp, w_ready, j + 1 - KT)
                    sp.dma_start(w_slots[k], w_in[k * P:(k + 1) * P, w_at[c]:w_at[c] + HW]).then_inc(w_loaded[k], 16)
                if c == 0:
                    sp.dma_start(lbt[:, 0, :], lb_logits).then_inc(lb_loaded, 16)
                    sp.dma_start(hgnw[:, :], hg_norm_w.to_broadcast([P, P])).then_inc(lb_loaded, 16)
                    load_x(tile(0, 1))
            for b in range(4):
                sp.wait_ge(w_ready, 3 * KT + 5 + b)
                sp.dma_start(by_head(ring[b]), by_key(state[b])).then_inc(st_loaded[b], 16)
            load_x(tile(0, 2))
            load_x(tile(0, 3))
            for b in range(NS):
                sp.wait_ge(s1_done, b + 1)
                sp.dma_start(by_key(new_state_sample[b]), by_head(ring[b % 4])).then_inc(s1_stored[b % 4], 16)
                if b + 4 < NS:
                    sp.wait_ge(s1_stored[b % 4], 16)
                    sp.wait_ge(so_mm, b + 1)
                    sp.dma_start(by_head(ring[b % 4]), by_key(state[b + 4])).then_inc(st_loaded[b % 4], 16)
            sp.wait_ge(mix_done, 1)
            sp.dma_start(mixed_sample[:, HW:D], MIX_S[sample_rows, :]).then_inc(mix_stored, 16)
            load_x(tile(0, 4))
            with sp.Fori(*LOOP) as it:
                for c in range(2):
                    load_x(tile(it, c + 3))
                    store_mixed(tile(it, c - 1))
            for n in range(LAST, TILES):
                store_mixed(tile(0, n))
            sp.wait_ge(s_new, TILES)
            sp.dma_start(by_key(new_state), by_head(S)).then_inc(rest_stored, 16)
            sp.wait_ge(rest_stored, 16)
            for i in range(4):
                sp.wait_ge(s1_stored[i], 32)
            sp.wait_ge(mix_stored, 16 * TILES)

        @block.gpsimd
        def _(pool):
            pool.memset(half_power[:, :], -0.5).then_inc(power_set, 1)
            pool.wait_ge(power_set, 1)

            def x_rstd(t):
                pool.wait_ge(var_done, t.n + 1)
                wait(pool, x_scaled, t.n)
                pool.tensor_tensor(rstd[:, :], var[:, :], half_power[:, 0:1], ALU.pow).then_inc(rstd_done, 1)

            def g_scale(t):
                pool.wait_ge(g_silu, t.n + 1)
                g = G[t.slot][:, :].rearrange("p (h v) -> p h v", h=HH)
                pool.tensor_tensor(g, g, hgnw[:, :].unsqueeze(1).to_broadcast([P, HH, P]), ALU.mult).then_inc(g_done, 1)

            def o_rstd(n):
                pool.wait_ge(ovar_done, n + 1)
                pool.tensor_tensor(orstd[:, :], ovar[:, :], half_power[:, :], ALU.pow).then_inc(orstd_done, 1)

            def k_levels(t, first, end):
                for v in range(first, end):
                    b = 2 ** v
                    if v:
                        pool.wait_ge(totals, 7 * (t.n - 1) + v)
                        pool.wait_ge(k_lev, 7 * (t.n - 1) + v)
                        pool.wait_ge(lev_mm, 8 * (t.n - 1) + v + 2)
                    else:
                        pool.wait_ge(fk_done, t.n + 1)
                        wait(pool, k_turned, t.n - 1)
                    old, new = blocks(K[t.slot] if v else Kz[:, :], b), blocks(K[t.slot], b)
                    right = tot(b).rearrange("p (n two) -> p n two", two=2)[:, :, 1]
                    ins = pool.tensor_tensor(new[:, :, 0, :], old[:, :, 0, :],
                                             right.unsqueeze(2).to_broadcast([P, HW // (2 * b), b]), ALU.mult)
                    if v == 0:
                        ins = pool.tensor_copy(new[:, :, 1, :], old[:, :, 1, :])
                    ins.then_inc(k_lev, 1)

            x_rstd(tile(0, 0))
            x_rstd(tile(0, 1))
            pool.wait_ge(lb_loaded, 32)
            g_scale(tile(0, 0))
            x_rstd(tile(0, 2))
            o_rstd(0)

            def iteration(t0, t2, tail=True, more=True, last=False):
                k_levels(t0, 0, 1)
                g_scale(t0)
                k_levels(t0, 1, 2)
                if last:
                    k_levels(t0, 2, 3)
                if tail:
                    o_rstd(t0.n - 1)
                k_levels(t0, 3 if last else 2, 4)
                if more:
                    x_rstd(t2)
                k_levels(t0, 4, 7)

            iteration(tile(0, 1), tile(0, 3), tail=False)
            with pool.Fori(*LOOP) as it:
                for c in range(2):
                    iteration(tile(it, c), tile(it, c + 2))
            for n in range(LAST + 1, TILES):
                iteration(tile(0, n), tile(0, n + 2), more=n + 2 < TILES, last=n + 1 == TILES)
            o_rstd(TILES - 1)

        @block.scalar
        def _(act):
            def square_x(t):
                act.wait_ge(x_loaded[t.slot], 16 * (t.half + 1 + (t.slot == 0)))
                wait(act, var_done, t.n)
                wait(act, x_squared, t.n)
                act.activation(junk_x[:, :], X[t.slot][:, :], ACT.Square, accum_out=ss[:, :]).then_inc(x_squared, 1)

            def split_high(t, a):
                act.wait_ge(xt, 2 * t.n + a + 1)
                act.activation(half(h_hi[t.slot], a), x_bank(t, a)[:, :], ACT.Copy).then_inc(h_high, 1)

            def gates(t):
                act.wait_ge(zt, t.n + 1)
                act.activation(F[:, :], bank_t[:, :], ACT.Sigmoid)
                act.activation(Kz[:, :], bank_t[:, :], ACT.Sigmoid, scale=-1.0).then_inc(fk_sig, 1)

            def q_sigmoid(t):
                act.wait_ge(q_proj, t.n + 1)
                wait(act, g_silu, t.n)
                act.activation(q_sig[:, :], qg_bank(t)[:, :], ACT.Sigmoid).then_inc(q_sigm, 1)

            def g_sigmoid(t):
                act.wait_ge(g_proj, t.n + 1)
                act.wait_ge(q_silu, t.n + 1)
                act.activation(q_sig[:, :], qg_bank(t)[:, :], ACT.Sigmoid).then_inc(g_sigm, 1)

            def v_copy(t):
                act.wait_ge(i_proj, t.n + 1)
                wait(act, s_mm, t.n - 1)
                act.activation(V[t.slot][:, :], fi_bank(t)[:, :], ACT.Copy).then_inc(v_copied, 1)

            def q0_copy(t):
                act.wait_ge(qt, t.n + 1)
                act.activation(Qz[:, :], bank_t[:, :], ACT.Copy).then_inc(q0_done, 1)

            def k_copy(n):
                act.wait_ge(k_turned, n + 1)
                wait(act, s_mm, n)
                act.activation(KN[:, :], bank_t[:, :], ACT.Copy).then_inc(k_nat, 1)

            def square_o(n, rows=P):
                act.wait_ge(o_mm, n + 1)
                wait(act, ovar_done, n)
                wait(act, o_squared, n)
                for h in range(HH):
                    ins = act.activation(junk_o[0:rows, h * P:(h + 1) * P], bank_o[0:rows, h * P:(h + 1) * P], ACT.Square,
                                         accum_out=oss[0:rows, h:h + 1])
                ins.then_inc(o_squared, 1)

            def split_weights(c):
                for k in range(KT):
                    act.wait_ge(w_loaded[k], 16 * (c + 1))
                    act.activation(w_hi[:, k, c * HW:(c + 1) * HW], w_slots[k], ACT.Copy, scale=nw[:, k:k + 1]).then_inc(w_high, 1)

            square_x(tile(0, 0))
            split_high(tile(0, 0), 0)
            split_high(tile(0, 0), 1)
            act.wait_ge(nw_loaded, 16)
            split_weights(0)
            act.wait_ge(lbd, 1)
            act.activation(lbt[:, 2, :], lbt[:, 1, :], ACT.Exp).then_inc(lbe, 1)
            square_x(tile(0, 1))
            split_weights(1)
            split_high(tile(0, 1), 0)
            split_high(tile(0, 1), 1)
            q_sigmoid(tile(0, 0))
            gates(tile(0, 0))
            split_weights(2)
            q0_copy(tile(0, 0))
            v_copy(tile(0, 0))
            split_weights(3)
            g_sigmoid(tile(0, 0))
            q_sigmoid(tile(0, 1))
            v_copy(tile(0, 1))
            k_copy(0)
            square_x(tile(0, 2))
            split_high(tile(0, 2), 0)
            split_high(tile(0, 2), 1)
            act.wait_ge(s1_done, NS)
            gates(tile(0, 1))
            act.wait_ge(qm_done, 1)
            q0_copy(tile(0, 1))
            square_o(0, 64)

            def iteration(t0, t1, t2, tail=True, ahead=True, more=True):
                if ahead and tail:
                    split_high(t1, 1)
                g_sigmoid(t0)
                if more:
                    square_x(t2)
                if tail:
                    k_copy(t0.n - 1)
                    square_o(t0.n - 1)
                if ahead:
                    act.wait_ge(totals, 7 * (t0.n - 1) + 1)
                    act.wait_ge(k_lev, 7 * (t0.n - 1) + 1)
                    act.wait_ge(q_lev, 8 * (t0.n - 1) + 1)
                    act.wait_ge(lev_mm, 8 * (t0.n - 1) + 2)
                    gates(t1)
                    q_sigmoid(t1)
                    v_copy(t1)
                    q0_copy(t1)
                if more:
                    split_high(t2, 0)

            iteration(tile(0, 1), tile(0, 2), tile(0, 3), tail=False)
            with act.Fori(*LOOP) as it:
                for c in range(2):
                    iteration(tile(it, c), tile(it, c + 1), tile(it, c + 2))
            for n in range(LAST + 1, TILES):
                iteration(tile(0, n), tile(0, n + 1), tile(0, n + 2), ahead=n + 1 < TILES, more=n + 2 < TILES)
            square_o(TILES - 1)
            k_copy(TILES - 1)

        @block.vector
        def _(dve):
            dve.memset(X[0][:, :], 0.0).then_inc(x_zeroed, 1)

            def x_var(t):
                dve.wait_ge(x_squared, t.n + 1)
                wait(dve, rstd_done, t.n)
                dve.tensor_scalar(var[:, :], ss[:, :], 1.0 / D, EPS, ALU.mult, ALU.add).then_inc(var_done, 1)

            def x_scale(t):
                dve.wait_ge(rstd_done, t.n + 1)
                dve.tensor_scalar(X[t.slot][:, :], X[t.slot][:, :], rstd[:, 0:1], None, ALU.mult).then_inc(x_scaled, 1)

            def split_low(t, a):
                dve.wait_ge(h_high, 2 * t.n + a + 1)
                dve.tensor_tensor(half(h_lo[t.slot], a), x_bank(t, a)[:, :], half(h_hi[t.slot], a).bitcast(F32), ALU.subtract).then_inc(h_low, 1)

            def z_copy(t):
                dve.wait_ge(f_proj, t.n + 1)
                wait(dve, zt, t.n)
                dve.tensor_copy(z_nat[:, :], fi_bank(t)[:, :]).then_inc(z_copied, 1)

            def q_mul(t):
                dve.wait_ge(q_sigm, t.n + 1)
                wait(dve, qt, t.n)
                dve.tensor_tensor(q_nat[:, :], qg_bank(t)[:, :], q_sig[:, :], ALU.mult).then_inc(q_silu, 1)

            def g_mul(t):
                dve.wait_ge(g_sigm, t.n + 1)
                dve.tensor_tensor(G[t.slot][:, :], qg_bank(t)[:, :], q_sig[:, :], ALU.mult).then_inc(g_silu, 1)

            def fk_affine(t):
                dve.wait_ge(fk_sig, t.n + 1)
                for h in range(HH):
                    f, k = F[:, h * P:(h + 1) * P], Kz[:, h * P:(h + 1) * P]
                    dve.tensor_scalar(k, k, oml[:, h:h + 1], None, ALU.mult)
                    dve.tensor_scalar(f, f, oml[:, h:h + 1], lb[:, h:h + 1], ALU.mult, ALU.add).then_inc(fk_aff, 1)
                dve.wait_ge(fk_aff, 4 * t.n + 4)
                dve.tensor_scalar(F[:, :], F[:, :], TINY, None, ALU.max).then_inc(fk_done, 1)

            def block_totals(t):
                dve.wait_ge(fk_done, t.n + 1)
                wait(dve, k_lev, 7 * (t.n - 1))
                for v in range(7):
                    b = 2 ** v
                    if v:
                        dve.wait_ge(totals, 7 * (t.n - 1) + v)
                    pair = tot(b).rearrange("p (n two) -> p n two", two=2)
                    out = tot(2 * b) if b < 64 else TE[t.slot][:, :]
                    dve.tensor_tensor(out, pair[:, :, 0], pair[:, :, 1], ALU.mult).then_inc(totals, 1)

            def q_levels(t, first, end):
                for v in range(first, end):
                    if v == 0:
                        dve.wait_ge(q0_done, t.n + 1)
                        wait(dve, o_mm, t.n - 1)
                        dve.tensor_tensor(Q[t.slot], Qz[:, :], F[:, :], ALU.mult).then_inc(q_lev, 1)
                        continue
                    b = 2 ** (v - 1)
                    dve.wait_ge(q_lev, 8 * (t.n - 1) + v)
                    dve.wait_ge(lev_mm, 8 * (t.n - 1) + v + 1)
                    right_half = blocks(Q[t.slot], b)[:, :, 1, :]
                    left = tot(b).rearrange("p (n two) -> p n two", two=2)[:, :, 0]
                    dve.tensor_tensor(right_half, right_half, left.unsqueeze(2).to_broadcast([P, HW // (2 * b), b]),
                                      ALU.mult).then_inc(q_lev, 1)

            def near_mask(t, part):
                dve.wait_ge(lev_mm, 8 * (t.n - 1) + 3 * part + 3)
                wait(dve, near_summed, t.n - 1)
                products = (near_a, near_b)[part][:, 0:384].rearrange("p (h l) -> p h l", h=HH)
                mask = (mask_a, mask_b)[part].unsqueeze(1).to_broadcast([P, HH, 96])
                dve.tensor_tensor(PR[:, part, :, :, :].rearrange("p h l c -> p h (l c)"), products, mask,
                                  ALU.mult).then_inc(near_masked, 1)

            def near_sum(t):
                dve.wait_ge(near_masked, 2 * t.n)
                dve.tensor_tensor(PR[:, 0, :, :, :].rearrange("p h l c -> p (h l c)"),
                                  PR[:, 0, :, :, :].rearrange("p h l c -> p (h l c)"),
                                  PR[:, 1, :, :, :].rearrange("p h l c -> p (h l c)"), ALU.add).then_inc(near_added, 1)
                dve.wait_ge(near_added, 2 * t.n - 1)
                dve.tensor_tensor(PR[:, 1, :, 0, :], PR[:, 0, :, 0, :], PR[:, 0, :, 1, :], ALU.add).then_inc(near_added, 1)
                dve.wait_ge(near_added, 2 * t.n)
                dve.wait_ge(o_mm, t.n)
                for j in range(4):
                    r = slice(32 * j, 32 * j + 32)
                    ins = dve.tensor_tensor(A[r, :, r], PR[r, 1, :, 0, :], PR[r, 0, :, 2, :], ALU.add)
                ins.then_inc(near_summed, 1)

            def far_copy(t):
                dve.wait_ge(lev_mm, 8 * t.n)
                for j in (0, 2):
                    dve.tensor_copy(A[32 * j:32 * j + 32, :, 32 * j + 32:32 * j + 64],
                                    far[32 * j:32 * j + 32, 0:P].rearrange("p (h c) -> p h c", h=HH))
                dve.tensor_copy(A[0:64, :, 64:P], far[0:64, P:3 * P].rearrange("p (h c) -> p h c", h=HH)).then_inc(far_copied, 1)

            def state_step(t):
                dve.wait_ge(s_mm, t.n + 1)
                dve.wait_ge(o_mm, t.n + 1)
                dve.wait_ge(s_new, t.n)
                for h in range(HH):
                    c = slice(h * P, (h + 1) * P)
                    ins = dve.scalar_tensor_tensor(S[:, c], S[:, c], TE[t.slot][:, h:h + 1], bank_s[:, c], ALU.mult, ALU.add)
                ins.then_inc(s_new, 1)

            def o_var(n):
                dve.wait_ge(o_squared, n + 1)
                wait(dve, orstd_done, n)
                dve.tensor_scalar(ovar[:, :], oss[:, :], 1.0 / P, EPS, ALU.mult, ALU.add).then_inc(ovar_done, 1)

            def mix(n, g, out, rows):
                dve.wait_ge(orstd_done, n + 1)
                dve.wait_ge(g_done, n + 1)
                for h in range(HH):
                    c = slice(h * P, (h + 1) * P)
                    ins = dve.scalar_tensor_tensor(out[0:rows, c], bank_o[0:rows, c], orstd[0:rows, h:h + 1], g[0:rows, c],
                                                   ALU.mult, ALU.mult)
                ins.then_inc(mix_done, 1)

            def split_weights(c):
                for k in range(KT):
                    dve.wait_ge(w_high, KT * c + k + 1)
                    cols = slice(c * HW, (c + 1) * HW)
                    dve.scalar_tensor_tensor(w_lo[:, k, cols], w_slots[k], nw[:, k:k + 1], w_hi[:, k, cols].bitcast(F32),
                                             ALU.mult, ALU.subtract).then_inc(w_ready, 1)

            dve.memset(A[:, :, :], 0.0)
            dve.memset(oss[:, :], 0.0).then_inc(a_zeroed, 1)
            dve.wait_ge(a_zeroed, 1)
            x_var(tile(0, 0))
            x_scale(tile(0, 0))
            split_low(tile(0, 0), 0)
            split_low(tile(0, 0), 1)
            dve.wait_ge(nw_loaded, 16)
            split_weights(0)
            dve.wait_ge(lb_loaded, 32)
            dve.tensor_tensor(lbt[:, 1, :], lbt[:, 0, :], lbt[:, 0, :], ALU.subtract).then_inc(lbd, 1)
            dve.wait_ge(lbe, 1)
            dve.reciprocal(lbt[:, 3, :], lbt[:, 2, :]).then_inc(lbd, 1)
            dve.wait_ge(lbd, 2)
            dve.tensor_tensor(lbt[:, 1, :], lbt[:, 2, :], lbt[:, 3, :], ALU.mult).then_inc(lbd, 1)
            dve.wait_ge(lbd, 3)
            dve.tensor_tensor(lb, lbt[:, 1, :], lbt[:, 1, :], ALU.subtract).then_inc(lbd, 1)
            dve.wait_ge(lbd, 4)
            dve.tensor_scalar(oml, lb, -1.0, 1.0, ALU.mult, ALU.add).then_inc(lbd, 1)
            dve.wait_ge(lbd, 5)
            x_var(tile(0, 1))
            x_scale(tile(0, 1))
            split_weights(1)
            split_low(tile(0, 1), 0)
            split_low(tile(0, 1), 1)
            z_copy(tile(0, 0))
            q_mul(tile(0, 0))
            split_weights(2)
            fk_affine(tile(0, 0))
            split_weights(3)
            z_copy(tile(0, 1))
            dve.wait_ge(w_ready, 4 * KT)
            dve.memset(LV[:, :, :], 0.0).then_inc(qm_zeroed, 1)
            dve.wait_ge(q0_done, 1)
            dve.wait_ge(qm_zeroed, 1)
            dve.tensor_copy(qm[:, :, SROW:SROW + 65 * (NS - 1) + 1:65],
                            Qz[:, :].rearrange("p (h t) -> p h t", h=HH)[:, :, SROW:SROW + NS]).then_inc(qm_done, 1)
            g_mul(tile(0, 0))
            q_mul(tile(0, 1))
            dve.wait_ge(fk_done, 1)
            meta_f = F[:, :].rearrange("p (h t) -> p h t", h=HH)
            meta_tot = TT[:, :].rearrange("p (h t) -> p h t", h=HH)
            at = 0
            for v in range(4):
                b = 2 ** v
                m = META // (2 * b)
                decays = meta_f[:, :, 0:META] if v == 0 else meta_tot[:, :, at:at + 2 * m]
                pair = decays.rearrange("p h (n two) -> p h n two", two=2)
                if v:
                    dve.wait_ge(meta_k, 2 * v)
                for h in range(HH):
                    k = blocks(Kz[:, h * P:h * P + META], b)
                    ins = dve.tensor_tensor(k[:, :, 0, :], k[:, :, 0, :],
                                            pair[:, h, :, 1].unsqueeze(2).to_broadcast([P, m, b]), ALU.mult)
                ins.then_inc(meta_k, 1)
                at = at + 2 * m if v else 0
                if v < 3:
                    dve.tensor_tensor(meta_tot[:, :, at:at + m], pair[:, :, :, 0], pair[:, :, :, 1], ALU.mult).then_inc(meta_k, 1)
            def sample_key(b):
                dve.wait_ge(k_nat, 1)
                wait(dve, outer_mm, b - 1)
                dve.tensor_scalar(km[b % 2][sample_rows, :], KN[sample_rows, :], ident[sample_rows, SROW + b:SROW + b + 1], None,
                                  ALU.mult).then_inc(km_done, 1)

            def sample_state(b):
                dve.wait_ge(outer_mm, b + 1)
                dve.wait_ge(st_loaded[b % 4], 16 * (b // 4 + 1))
                for h in range(HH):
                    c = slice(h * P, (h + 1) * P)
                    ins = dve.scalar_tensor_tensor(ring[b % 4][:, c], ring[b % 4][:, c], F[:, h * P + SROW + b:h * P + SROW + b + 1],
                                                   outer_bank[b % 2][:, c], ALU.mult, ALU.add)
                ins.then_inc(s1_done, 1)

            dve.wait_ge(c_loaded, 16)
            sample_key(0)
            dve.wait_ge(s_mm, 1)
            dve.tensor_copy(S[:, :], bank_s[:, :]).then_inc(s_new, 1)
            for b in range(NS):
                if b + 1 < NS:
                    sample_key(b + 1)
                sample_state(b)
                if b == 0:
                    x_var(tile(0, 2))
                    x_scale(tile(0, 2))
                elif b in (3, 5):
                    split_low(tile(0, 2), (b - 3) // 2)
            fk_affine(tile(0, 1))
            o_var(0)
            mix(0, G[0], MIX_S, 64)

            def iteration(t0, t1, t2, last, tail=True, ahead=True, more=True):
                if ahead and tail:
                    split_low(t1, 1)
                block_totals(t0)
                q_levels(t0, 0, 1)
                g_mul(t0)
                q_levels(t0, 1, 2)
                if ahead:
                    z_copy(t1)
                q_levels(t0, 2, 3)
                if not ahead:
                    q_levels(t0, 3, 4)
                if tail:
                    state_step(last)
                    o_var(last.n)
                near_mask(t0, 0)
                if not ahead:
                    q_levels(t0, 4, 5)
                if tail:
                    if isinstance(last.n, int) and last.n < 3:
                        dve.wait_ge(s1_stored[3 if last.slot else 2], 32)
                    wait(dve, mix_stored, 16 * last.n)
                    mix(last.n, G[last.slot], MIX[last.slot], P)
                if ahead:
                    q_levels(t0, 3, 4)
                    q_mul(t1)
                    fk_affine(t1)
                    q_levels(t0, 4, 5)
                if more:
                    x_var(t2)
                    x_scale(t2)
                q_levels(t0, 5, 6)
                near_mask(t0, 1)
                near_sum(t0)
                q_levels(t0, 6, 7)
                if more:
                    split_low(t2, 0)
                q_levels(t0, 7, 8)
                far_copy(t0)

            iteration(tile(0, 1), tile(0, 2), tile(0, 3), None, tail=False)
            iteration_args = lambda it, c: (tile(it, c), tile(it, c + 1), tile(it, c + 2), tile(it, c - 1))
            dve.wait_ge(s1_stored[2], 32)
            dve.wait_ge(s1_stored[3], 32)
            with dve.Fori(*LOOP) as it:
                for c in range(2):
                    iteration(*iteration_args(it, c))
            for n in range(LAST + 1, TILES):
                iteration(*iteration_args(0, n), ahead=n + 1 < TILES, more=n + 2 < TILES)
            last = tile(0, TILES - 1)
            o_var(last.n)
            wait(dve, mix_stored, 16 * last.n)
            mix(last.n, G[last.slot], MIX[last.slot], P)
            state_step(last)

        @block.tensor
        def _(pe):
            def turn(out, source, sem, count=4):
                for j in range(count):
                    ins = pe.transpose(out[:, j * P:(j + 1) * P], source[:, j * P:(j + 1) * P], ident)
                ins.then_inc(sem, 1)

            def turn_x(t, a):
                pe.wait_ge(x_scaled, t.n + 1)
                turn(x_bank(t, a), X[t.slot][:, a * HW:(a + 1) * HW], xt)

            def project(t, out, c, halves, first=False):
                for a in halves:
                    for k in range(4 * a, 4 * a + 4):
                        if first:
                            pe.wait_ge(w_ready, KT * c + k + 1)
                            if (c, k) == (0, KT // 2):
                                pe.wait_ge(h_low, 2)
                        hi, lo = w_hi[:, k, c * HW:(c + 1) * HW], w_lo[:, k, c * HW:(c + 1) * HW]
                        pe.matmul(out[:, :], h_hi[t.slot][:, k, :], hi, start=(k == 0), stop=False)
                        pe.matmul(out[:, :], h_hi[t.slot][:, k, :], lo, start=False, stop=False)
                        ins = pe.matmul(out[:, :], h_lo[t.slot][:, k, :], hi, start=False, stop=(k == KT - 1))
                return ins

            def level(t, v):
                q = Q[t.slot] if v else Qz
                k = K[t.slot] if v > 1 else Kz
                if v == 0:
                    pe.wait_ge(q0_done, t.n + 1)
                    pe.wait_ge(fk_done, t.n + 1)
                    wait(pe, near_masked, 2 * (t.n - 1))
                else:
                    pe.wait_ge(q_lev, 8 * (t.n - 1) + v)
                    if v > 1:
                        pe.wait_ge(k_lev, 7 * (t.n - 1) + v - 1)
                if v == 6:
                    wait(pe, far_copied, t.n - 1)
                for h in range(HH):
                    if v < 6:
                        out = (near_a if v < 3 else near_b)
                        for j in range(4):
                            r = slice(32 * j, 32 * j + 32)
                            c = slice(h * P + 32 * j, h * P + 32 * j + 32)
                            at = (h * 3 + v % 3) * 32
                            ins = pe.matmul(out[r, at:at + 32], k[:, c], q[:, c], start=True, stop=True)
                    elif v == 6:
                        for j in (0, 2):
                            at = h * P + 32 * j
                            ins = pe.matmul(far[32 * j:32 * j + 32, 32 * h:32 * h + 32], k[:, at:at + 32],
                                            q[:, at + 32:at + 64], start=True, stop=True)
                    else:
                        ins = pe.matmul(far[0:64, P + 64 * h:P + 64 * h + 64], k[:, h * P:h * P + 64],
                                        q[:, h * P + 64:(h + 1) * P], start=True, stop=True)
                ins.then_inc(lev_mm, 1)

            def outputs(t):
                pe.wait_ge(q_lev, 8 * t.n)
                pe.wait_ge(near_summed, t.n)
                pe.wait_ge(far_copied, t.n)
                pe.wait_ge(s_new, t.n)
                pe.wait_ge(v_copied, t.n + 1)
                pe.wait_ge(mix_done, t.n)
                for h in range(HH):
                    c = slice(h * P, (h + 1) * P)
                    pe.matmul(bank_o[:, c], Q[t.slot][:, c], S[:, c], start=True, stop=False)
                    ins = pe.matmul(bank_o[:, c], A[:, h, :], V[t.slot][:, c], start=False, stop=True)
                ins.then_inc(o_mm, 1)

            def turn_k(t):
                pe.wait_ge(k_lev, 7 * t.n)
                turn(bank_t, K[t.slot], k_turned)

            def state_product(t):
                pe.wait_ge(k_nat, t.n + 1)
                for h in range(HH):
                    c = slice(h * P, (h + 1) * P)
                    ins = pe.matmul(bank_s[:, c], KN[:, c], V[t.slot][:, c], start=True, stop=True)
                ins.then_inc(s_mm, 1)

            pe.wait_ge(c_loaded, 16)
            t0, t1, t2 = tile(0, 0), tile(0, 1), tile(0, 2)
            turn_x(t0, 0)
            turn_x(t0, 1)
            pe.wait_ge(h_low, 1)
            project(t0, fi_bank(t0), 0, (0, 1), True).then_inc(f_proj, 1)
            turn_x(t1, 0)
            turn_x(t1, 1)
            project(t0, qg_bank(t0), 1, (0, 1), True).then_inc(q_proj, 1)
            pe.wait_ge(z_copied, 1)
            pe.wait_ge(h_low, 4)
            turn(bank_t, z_nat, zt)
            project(t1, fi_bank(t1), 0, (0, 1)).then_inc(f_proj, 1)
            project(t0, fi_bank(t0), 2, (0,), True)
            pe.wait_ge(q_silu, 1)
            pe.wait_ge(fk_sig, 1)
            turn(bank_t, q_nat, qt)
            project(t0, fi_bank(t0), 2, (1,), True).then_inc(i_proj, 1)
            project(t1, qg_bank(t1), 1, (0, 1)).then_inc(q_proj, 1)
            project(t0, qg_bank(t0), 3, (0, 1), True).then_inc(g_proj, 1)
            pe.wait_ge(z_copied, 2)
            project(t1, fi_bank(t1), 2, (0, 1)).then_inc(i_proj, 1)
            pe.wait_ge(meta_k, 7)
            pe.wait_ge(q0_done, 1)
            turn(bank_t, Kz, k_turned)

            def sample_outer(b):
                pe.wait_ge(km_done, b + 1)
                wait(pe, s1_done, b - 1)
                for h in range(HH):
                    c = slice(h * P, (h + 1) * P)
                    ins = pe.matmul(outer_bank[b % 2][:, c], km[b % 2][sample_rows, c], V[0][sample_rows, c], start=True, stop=True)
                ins.then_inc(outer_mm, 1)

            def sample_output(b):
                pe.wait_ge(s1_done, b + 1)
                pe.wait_ge(qm_done, 1)
                for h in range(HH):
                    ins = pe.matmul(bank_o[0:64, h * P:(h + 1) * P], qm[:, h, 64 * b:64 * b + 64], ring[b % 4][:, h * P:(h + 1) * P],
                                    start=(b == 0 and h == 0), stop=(b == NS - 1), skip_group_check=True)
                ins.then_inc(so_mm if b < NS - 1 else o_mm, 1)

            pe.wait_ge(k_nat, 1)
            for h in range(HH):
                c = slice(h * P, (h + 1) * P)
                ins = pe.matmul(bank_s[:, c], KN[0:META, c], V[0][0:META, c], start=True, stop=True)
            ins.then_inc(s_mm, 1)
            sample_outer(0)
            sample_outer(1)
            sample_output(0)
            pe.wait_ge(q_silu, 2)
            project(t1, qg_bank(t1), 3, (0,))
            sample_outer(2)
            sample_output(1)
            sample_outer(3)
            sample_output(2)
            turn_x(t2, 0)
            project(t1, qg_bank(t1), 3, (1,)).then_inc(g_proj, 1)
            for b in range(4, NS):
                sample_outer(b)
                sample_output(b - 1)
                if b == 5:
                    pe.wait_ge(h_low, 5)
                    turn_x(t2, 1)
            pe.wait_ge(h_low, 6)
            turn(bank_t, z_nat, zt)
            sample_output(NS - 1)
            pe.wait_ge(fk_sig, 2)
            turn(bank_t, q_nat, qt)

            def iteration(t0, t1, t2, last, tail=True, ahead=True, more=True):
                if ahead:
                    pe.wait_ge(v_copied, t0.n + 1)
                    pe.wait_ge(h_low, 2 * t1.n + 1)
                    project(t1, bank_a, 0, (0,))
                level(t0, 0)
                if ahead:
                    pe.wait_ge(h_low, 2 * t1.n + 2)
                    project(t1, bank_a, 0, (1,)).then_inc(f_proj, 1)
                level(t0, 1)
                if tail:
                    outputs(last)
                    if not ahead:
                        pe.wait_ge(q0_done, t0.n + 1)
                    turn_k(last)
                if ahead:
                    pe.wait_ge(g_silu, t0.n + 1)
                    project(t1, bank_b, 1, (0,))
                level(t0, 2)
                if tail:
                    state_product(last)
                if ahead:
                    pe.wait_ge(z_copied, t1.n + 1)
                    turn(bank_t, z_nat, zt)
                    project(t1, bank_b, 1, (1,)).then_inc(q_proj, 1)
                level(t0, 3)
                if ahead:
                    project(t1, bank_a, 2, (0,))
                level(t0, 4)
                if ahead:
                    project(t1, bank_a, 2, (1,)).then_inc(i_proj, 1)
                level(t0, 5)
                if ahead:
                    pe.wait_ge(q_silu, t1.n + 1)
                    pe.wait_ge(fk_sig, t1.n + 1)
                    turn(bank_t, q_nat, qt)
                    project(t1, bank_b, 3, (0,))
                if more:
                    pe.wait_ge(q0_done, t1.n + 1)
                    turn_x(t2, 0)
                level(t0, 6)
                if ahead:
                    project(t1, bank_b, 3, (1,)).then_inc(g_proj, 1)
                level(t0, 7)
                if more:
                    pe.wait_ge(h_low, 2 * t2.n + 1)
                    turn_x(t2, 1)

            iteration(tile(0, 1), tile(0, 2), tile(0, 3), None, tail=False)
            with pe.Fori(*LOOP) as it:
                for c in range(2):
                    iteration(tile(it, c), tile(it, c + 1), tile(it, c + 2), tile(it, c - 1))
            for n in range(LAST + 1, TILES):
                iteration(tile(0, n), tile(0, n + 1), tile(0, n + 2), tile(0, n - 1), ahead=n + 1 < TILES, more=n + 2 < TILES)
            last = tile(0, TILES - 1)
            outputs(last)
            turn_k(last)
            state_product(last)


def attention_pass(nc, x_prompt, x_sample, meta_tokens, w_in, norm_w, q_norm_w, k_norm_w, sinks, sinks_rows, consts, masks,
                   win_k, win_v, meta_k, meta_v, sample_o, mixed, mixed_sample,
                   new_win_k, new_win_v, new_meta_k, new_meta_v, new_win_k_sample, new_win_v_sample):
    with ExitStack() as ctx:
        def sb(name, shape, dt=F32):
            return ctx.enter_context(nc.sbuf_tensor("a_" + name, shape, dt))

        def psum(name, shape):
            return ctx.enter_context(nc.psum_tensor("a_" + name, shape, F32))

        def sem(name):
            return nc.alloc_semaphore(name="a_" + name)

        KV = 2 * KVH * HD
        W_AT = [0, KV, KV + HW]
        W_COLS = [KV, HW, HW]
        w_hi = sb("w_hi", [P, KT, ATT_COLS], F32R)
        w_lo = sb("w_lo", [P, KT, ATT_COLS], F32R)
        ws = sb("ws", [P, KT, HW])
        ident = sb("ident", [P, P])
        hidden = sb("hidden", [P, 3, KEYS])
        nw = sb("nw", [P, KT])
        qnw = sb("qnw", [P, HD])
        knw = sb("knw", [P, HD])
        sink = sb("sink", [P, AH])
        neg_sink = sb("neg_sink", [P, AH])
        half_power = sb("half_power", [P, AH])
        X = [sb(f"x{i}", [P, D]) for i in range(2)]
        h_hi = [sb(f"h_hi{i}", [P, KT, P], F32R) for i in range(2)]
        h_lo = [sb(f"h_lo{i}", [P, KT, P], F32R) for i in range(2)]
        junk_x = sb("junk_x", [P, D], BF16)
        ss, var, rstd = sb("ss", [P, 1]), sb("var", [P, 1]), sb("rstd", [P, 1])
        sq_k = sb("sq_k", [P, KVH * HD])
        sq_q = sb("sq_q", [P, HW])
        kss, kvar, krstd = sb("kss", [P, KVH]), sb("kvar", [P, KVH]), sb("krstd", [P, KVH])
        qss, qvar, qrstd = sb("qss", [P, AH]), sb("qvar", [P, AH]), sb("qrstd", [P, AH])
        k_nat = sb("k_nat", [P, KVH * HD])
        v_nat = sb("v_nat", [P, KVH * HD])
        q_nat = sb("q_nat", [P, HW])
        KS = sb("ks", [P, KVH, 4, HD], F32R)
        QS = sb("qs", [P, AH, 2, HD], F32R)
        KTS = sb("kts", [P, KVH, 2, KEYS], F32R)
        QT = sb("qt", [P, AH, P], F32R)
        V = [sb(f"v{i}", [P, KVH * HD]) for i in range(2)]
        V_meta = sb("v_meta", [META, KVH * HD])
        VMD = sb("vmd", [P, HW])
        SM = [sb(f"sm{i}", [P, 2, KEYS]) for i in range(2)]
        neg_m = sb("neg_m", [P, AH])
        row_sum, row_sum_meta = sb("row_sum", [P, AH]), sb("row_sum_meta", [P, AH])
        sink_in, sink_e = sb("sink_in", [P, AH]), sb("sink_e", [P, AH])
        den, rden = sb("den", [P, AH]), sb("rden", [P, AH])
        PRB = [sb(f"prb{i}", [P, 2, 2 * P]) for i in range(2)]
        PM = sb("pm", [P, AH, META])
        PTS = sb("pts", [P, 2, 2 * P])
        PMT = sb("pmt", [P, P])
        G = [sb(f"g{i}", [P, HW]) for i in range(2)]
        g_exp = sb("g_exp", [P, HW])
        g_inv = sb("g_inv", [P, HW])
        o_nat = sb("o_nat", [P, HW])
        MIX = [sb(f"mix{i}", [P, HW]) for i in range(2)]
        KW, VW = sb("kw", [P, NS, KVH * HD]), sb("vw", [P, NS, KVH * HD])
        KM, VM = sb("km", [META, NS, KVH * HD]), sb("vm", [META, NS, KVH * HD])
        KTW = sb("ktw", [P, NS, P + META])
        QZ, PZ, PZM = sb("qz", [P, 72 * NS]), sb("pz", [P, 72 * NS]), sb("pzm", [META, 72 * NS])
        s_sink, s_neg, s_m = sb("s_sink", [64, 1]), sb("s_neg", [64, 1]), sb("s_m", [64, 1])
        s_sum, s_e, s_in, s_den, s_rden = (sb("s_" + x, [64, 1]) for x in ("sum", "e", "in", "den", "rden"))
        s_p = sb("s_p", [64, P + META])
        s_o = sb("s_o", [64, KVH * HD])
        s_nat = sb("s_nat", [64, HW])

        bank_p = [psum("bank_a", [P, 512]), psum("bank_b", [P, 512])]
        bank_t, bank_o = psum("bank_t", [P, 512]), psum("bank_o", [P, 512])
        sc, pt = psum("sc", [P, 2, 512]), psum("pt", [P, 2, 512])

        c_loaded, nw_loaded, sink_loaded = sem("c_loaded"), sem("nw_loaded"), sem("sink_loaded")
        sums_added, v_meta_spread, max_begun = sem("sums_added"), sem("v_meta_spread"), sem("max_begun")
        x_zeroed, power_set, sink_negated, buffers_zeroed = sem("x_zeroed"), sem("power_set"), sem("sink_negated"), sem("buffers_zeroed")
        w_loaded = [sem(f"w_loaded{i}") for i in range(KT)]
        w_high, w_ready = sem("w_high"), sem("w_ready")
        x_loaded = [sem(f"x_loaded{i}") for i in range(2)]
        x_squared, var_done, rstd_done, x_scaled = sem("x_squared"), sem("var_done"), sem("rstd_done"), sem("x_scaled")
        xt, h_high, h_low = sem("xt"), sem("h_high"), sem("h_low")
        kv_proj, q_proj, g_proj = sem("kv_proj"), sem("q_proj"), sem("g_proj")
        k_squared, k_summed, k_var, k_rstd, k_normed, k_high, k_low = (sem("k_" + x) for x in
            ("squared", "summed", "var", "rstd", "normed", "high", "low"))
        q_squared, q_summed, q_var, q_rstd, q_normed, q_done, q_high, q_low = (sem("q_" + x) for x in
            ("squared", "summed", "var", "rstd", "normed", "done", "high", "low"))
        v_copied, v_placed, k_turned, k_placed, q_turned, q_placed = (sem(x) for x in
            ("v_copied", "v_placed", "k_turned", "k_placed", "q_turned", "q_placed"))
        g_copied, g_plus, g_recip, g_ready = sem("g_copied"), sem("g_plus"), sem("g_recip"), sem("g_ready")
        scored, m_ready, exped, p_turned, p_placed, pv_done, o_ready = (sem(x) for x in
            ("scored", "m_ready", "exped", "p_turned", "p_placed", "pv_done", "o_ready"))
        sink_added, sink_exped, den_done, rden_done, o_normed, mix_done = (sem(x) for x in
            ("sink_added", "sink_exped", "den_done", "rden_done", "o_normed", "mix_done"))
        mix_stored = sem("mix_stored")
        cache_loaded, new_row, rest_stored, meta_stored = sem("cache_loaded"), sem("new_row"), sem("rest_stored"), sem("meta_stored")
        sk_turned, sk_placed, sq_turned, sq_placed = sem("sk_turned"), sem("sk_placed"), sem("sq_turned"), sem("sq_placed")
        s_scored, s_step, s_exped, sp_turned, sp_placed = sem("s_scored"), sem("s_step"), sem("s_exped"), sem("sp_turned"), sem("sp_placed")
        s_pv, s_scratch, s_back = sem("s_pv"), sem("s_scratch"), sem("s_back")

        FIRST, LAST = 2, TILES - 4
        LOOP = (FIRST // 2, (LAST + 1) // 2)
        s_rows = slice(SROW, SROW + NS)

        def heads(ap):
            return ap.rearrange("p (h d) -> p h d", d=HD)

        def first_tile(t):
            return isinstance(t.n, int) and t.n == 0

        def kv_bank(t):
            return pt[:, 0, :] if first_tile(t) else bank_p[t.slot]

        def q_bank(t):
            return pt[:, 1, :] if first_tile(t) else bank_p[1 - t.slot]

        def half(buffer, a):
            return buffer[:, 4 * a:4 * a + 4, :].rearrange("p k t -> p (k t)")

        def x_bank(t, a):
            if isinstance(t.n, int) and t.n < 2 and a == 1:
                return (bank_o, sc[:, 0, :])[t.n]
            return bank_t

        block = ctx.enter_context(nc.Block())

        @block.sync
        def _(sp):
            sp.dma_start(nw[:, :], norm_w).then_inc(nw_loaded, 16)
            sp.wait_ge(x_zeroed, 1)
            sp.dma_start(X[0][0:META, :], meta_tokens).then_inc(x_loaded[0], 16)
            sp.dma_start(X[0][s_rows, :], x_sample).then_inc(x_loaded[0], 16)
            sp.dma_start(ident[:, :], consts[:, 0:P]).then_inc(c_loaded, 16)

            def load_x(t):
                wait(sp, xt, 2 * t.n - 2)
                sp.dma_start(X[t.slot][:, :], rows_of(x_prompt, t)).then_inc(x_loaded[t.slot], 16)

            def store_mixed(t):
                sp.wait_ge(mix_done, t.n + 1)
                sp.dma_start(mixed[bass.ds((t.n - 1) * P, P), 0:HW], MIX[t.slot][:, :]).then_inc(mix_stored, 16)

            w_from = [HW, 0, HW + KV]
            for c in range(3):
                for k in range(KT):
                    j = KT * c + k
                    wait(sp, w_ready, j + 1 - KT)
                    sp.dma_start(ws[:, k, 0:W_COLS[c]], w_in[k * P:(k + 1) * P, w_from[c]:w_from[c] + W_COLS[c]]).then_inc(w_loaded[k], 16)
                    if (c, k) == (0, 3):
                        load_x(tile(0, 1))
                if c == 0:
                    sp.dma_start(qnw[:, :], q_norm_w.to_broadcast([P, HD])).then_inc(sink_loaded, 16)
                    sp.dma_start(knw[:, :], k_norm_w.to_broadcast([P, HD])).then_inc(sink_loaded, 16)
                    sp.dma_start(sink[:, :], sinks.to_broadcast([P, AH])).then_inc(sink_loaded, 16)
                    sp.dma_start(s_sink[:, :], sinks_rows).then_inc(sink_loaded, 16)
                    sp.dma_start(hidden[:, :, :], masks).then_inc(sink_loaded, 16)
                    load_x(tile(0, 2))
                    sp.dma_start(KW[0:P - 1, :, :], win_k[:, 1:P, :].rearrange("b s c -> s b c")).then_inc(cache_loaded, 16)
                    sp.dma_start(VW[0:P - 1, :, :], win_v[:, 1:P, :].rearrange("b s c -> s b c")).then_inc(cache_loaded, 16)
                    sp.dma_start(KM[:, :, :], meta_k.rearrange("b s c -> s b c")).then_inc(cache_loaded, 16)
                    sp.dma_start(VM[:, :, :], meta_v.rearrange("b s c -> s b c")).then_inc(cache_loaded, 16)
            sp.wait_ge(v_placed, 1)
            sp.wait_ge(buffers_zeroed, 1)
            for h in range(AH):
                kv = h // (AH // KVH)
                sp.dma_start(VMD[h * META:(h + 1) * META, h * HD:(h + 1) * HD], V_meta[:, kv * HD:(kv + 1) * HD]).then_inc(v_meta_spread, 16)
            sp.wait_ge(new_row, 32)
            sp.dma_start(new_win_k_sample.rearrange("b s c -> s b c"), KW[:, :, :]).then_inc(rest_stored, 16)
            sp.dma_start(new_win_v_sample.rearrange("b s c -> s b c"), VW[:, :, :]).then_inc(rest_stored, 16)
            load_x(tile(0, 3))
            sp.wait_ge(o_normed, 1)
            sp.dma_start(sample_o, s_o[:, :]).then_inc(s_scratch, 16)
            sp.wait_ge(s_scratch, 16)
            for kv in range(KVH):
                src = sample_o.rearrange("(b x g) (y d) -> x y b g d", b=NS, x=KVH, y=KVH)[kv, kv]
                dst = s_nat[s_rows, kv * HW // 2:(kv + 1) * HW // 2].rearrange("b (g d) -> b g d", d=HD)
                sp.dma_start(dst, src).then_inc(s_back, 16)
            load_x(tile(0, 4))
            sp.wait_ge(mix_done, 1)
            sp.dma_start(mixed_sample[:, 0:HW], s_nat[s_rows, :]).then_inc(mix_stored, 16)
            with sp.Fori(*LOOP) as it:
                for c in range(2):
                    load_x(tile(it, c + 3))
                    store_mixed(tile(it, c - 1))
            for n in range(LAST, TILES):
                store_mixed(tile(0, n))
            sp.dma_start(new_win_k, k_nat[:, :]).then_inc(rest_stored, 16)
            sp.dma_start(new_win_v, v_nat[:, :]).then_inc(rest_stored, 16)
            sp.wait_ge(rest_stored, 4 * 16)
            sp.wait_ge(meta_stored, 2 * 16)
            sp.wait_ge(mix_stored, 16 * TILES)

        @block.gpsimd
        def _(pool):
            pool.memset(QZ[:, :], 0.0)
            pool.memset(PZ[:, :], 0.0)
            pool.memset(PZM[:, :], 0.0)
            pool.memset(s_nat[:, :], 0.0)
            pool.memset(VMD[:, :], 0.0)
            pool.memset(KTS[:, :, :, :].bitcast(F32), 0.0).then_inc(buffers_zeroed, 1)
            pool.memset(half_power[:, :], -0.5).then_inc(power_set, 1)
            pool.wait_ge(power_set, 1)

            def x_rstd(t):
                pool.wait_ge(var_done, t.n + 1)
                wait(pool, x_scaled, t.n)
                pool.tensor_tensor(rstd[:, :], var[:, :], half_power[:, 0:1], ALU.pow).then_inc(rstd_done, 1)

            def k_rstd_of(t):
                pool.wait_ge(k_var, t.n + 1)
                wait(pool, k_normed, t.n)
                pool.tensor_tensor(krstd[:, :], kvar[:, :], half_power[:, 0:KVH], ALU.pow).then_inc(k_rstd, 1)

            def q_rstd_of(t):
                pool.wait_ge(q_var, t.n + 1)
                wait(pool, q_normed, t.n)
                pool.tensor_tensor(qrstd[:, :], qvar[:, :], half_power[:, :], ALU.pow).then_inc(q_rstd, 1)

            def q_weight(t):
                pool.wait_ge(q_normed, t.n + 1)
                if isinstance(t.n, int) and t.n == 0:
                    by_group = q_nat[:, :].rearrange("p (x g d) -> p x g d", x=KVH, d=HD)
                    side_by_side = o_nat[:, :].rearrange("p (g x d) -> p x g d", x=KVH, d=HD)
                    weight = qnw[:, :].unsqueeze(1).unsqueeze(1).to_broadcast([P, KVH, AH // KVH, HD])
                    pool.tensor_tensor(side_by_side, by_group, weight, ALU.mult).then_inc(q_done, 1)
                    return
                pool.tensor_tensor(heads(q_nat[:, :]), heads(q_nat[:, :]), qnw[:, :].unsqueeze(1).to_broadcast([P, AH, HD]),
                                   ALU.mult).then_inc(q_done, 1)

            def q_rest(t):
                pool.wait_ge(q_high, t.n)
                pool.tensor_tensor(QS[:, :, 1, :].bitcast(F32), heads(q_nat[:, :]), QS[:, :, 0, :].bitcast(F32),
                                   ALU.subtract).then_inc(q_low, 1)

            def mix(t):
                pool.wait_ge(o_normed, t.n + 1)
                pool.wait_ge(g_ready, t.n + 1)
                wait(pool, mix_stored, 16 * t.n)
                pool.tensor_tensor(MIX[t.slot][:, :], o_nat[:, :], G[t.slot][:, :], ALU.mult).then_inc(mix_done, 1)

            x_rstd(tile(0, 0))
            x_rstd(tile(0, 1))
            pool.wait_ge(sink_loaded, 5 * 16)
            k_rstd_of(tile(0, 0))
            k_rstd_of(tile(0, 1))
            q_rstd_of(tile(0, 0))
            q_weight(tile(0, 0))
            x_rstd(tile(0, 2))
            q_rstd_of(tile(0, 1))
            q_weight(tile(0, 1))
            q_rest(tile(0, 1))

            def iteration(t0, t1, t2, last, tail=True, ahead=True, more=True):
                if more:
                    x_rstd(t2)
                if tail:
                    mix(last)
                if ahead:
                    k_rstd_of(t1)
                    q_rstd_of(t1)
                    q_weight(t1)
                    q_rest(t1)

            iteration(tile(0, 1), tile(0, 2), tile(0, 3), None, tail=False)
            with pool.Fori(*LOOP) as it:
                for c in range(2):
                    iteration(tile(it, c), tile(it, c + 1), tile(it, c + 2), tile(it, c - 1))
            for n in range(LAST + 1, TILES):
                iteration(tile(0, n), tile(0, n + 1), tile(0, n + 2), tile(0, n - 1), ahead=n + 1 < TILES, more=n + 2 < TILES)
            mix(tile(0, TILES - 1))

        @block.scalar
        def _(act):
            def square_x(t):
                act.wait_ge(x_loaded[t.slot], 16 * (t.half + 1 + (t.slot == 0)))
                wait(act, var_done, t.n)
                wait(act, x_squared, t.n)
                act.activation(junk_x[:, :], X[t.slot][:, :], ACT.Square, accum_out=ss[:, :]).then_inc(x_squared, 1)

            def split_high(t, a):
                act.wait_ge(xt, 2 * t.n + a + 1)
                if not isinstance(t.n, int) or t.n >= 2:
                    act.wait_ge(g_proj, t.n - 1)
                act.activation(half(h_hi[t.slot], a), x_bank(t, a)[:, :], ACT.Copy).then_inc(h_high, 1)

            def keys_values(t):
                act.wait_ge(kv_proj, t.n + 1)
                wait(act, k_summed, t.n)
                act.activation(sq_k[:, :], kv_bank(t)[:, 0:P], ACT.Square).then_inc(k_squared, 1)
                wait(act, v_placed, t.n)
                if isinstance(t.n, int) and t.n == 1:
                    act.wait_ge(new_row, 32)
                    act.wait_ge(meta_stored, 2 * 16)
                act.activation(v_nat[:, :], kv_bank(t)[:, P:2 * P], ACT.Copy).then_inc(v_copied, 1)

            def square_q(t):
                act.wait_ge(q_proj, t.n + 1)
                wait(act, q_summed, t.n)
                act.activation(sq_q[:, :], q_bank(t)[:, :], ACT.Square).then_inc(q_squared, 1)

            def gate(t):
                act.wait_ge(g_proj, t.n + 1)
                wait(act, mix_done, t.n - 1)
                act.activation(G[t.slot][:, :], kv_bank(t)[:, :], ACT.Copy)
                wait(act, g_recip, 4 * t.n)
                act.activation(g_exp[:, :], kv_bank(t)[:, :], ACT.Exp, scale=-1.0).then_inc(g_copied, 1)

            def place_k(t):
                act.wait_ge(k_turned, t.n + 1)
                wait(act, scored, 4 * (t.n - 1))
                at = META + P * t.slot
                act.activation(KTS[:, :, :, at:at + P], bank_t[:, :].rearrange("p (a b t) -> p a b t", a=KVH, b=2),
                               ACT.Copy).then_inc(k_placed, 1)

            def place_q(t, a):
                act.wait_ge(q_turned, 2 * (t.n - 1) + a + 1)
                wait(act, scored, 4 * (t.n - 1))
                act.activation(QT[:, 4 * a:4 * a + 4, :].rearrange("p h t -> p (h t)"), bank_t[:, :], ACT.Copy).then_inc(q_placed, 1)

            def exps(t, j):
                act.wait_ge(m_ready, 4 * (t.n - 1) + j + 1)
                wait(act, p_turned, 4 * (t.n - 1) + j - (j > 0))
                if j == 0:
                    wait(act, den_done, t.n - 1)
                for i in range(2):
                    h = 2 * j + i
                    act.activation(PRB[j % 2][:, i, :], SM[j % 2][:, i, META:KEYS], ACT.Exp, bias=neg_m[:, h:h + 1], scale=-1.0,
                                   accum_out=row_sum[:, h:h + 1])
                    ins = act.activation(PM[:, h, :], SM[j % 2][:, i, 0:META], ACT.Exp, bias=neg_m[:, h:h + 1], scale=-1.0,
                                         accum_out=row_sum_meta[:, h:h + 1])
                ins.then_inc(exped, 1)

            def place_p(t, j):
                act.wait_ge(p_turned, 4 * (t.n - 1) + j + 1)
                wait(act, pv_done, 4 * (t.n - 1) + j)
                if j == 3:
                    act.activation(PMT[:, :], pt[:, 0, 2 * P:3 * P], ACT.Copy)
                act.activation(PTS[:, :, :], pt[:, :, 0:2 * P], ACT.Copy).then_inc(p_placed, 1)

            def sink_exp(t):
                act.wait_ge(sink_added, t.n)
                wait(act, den_done, t.n - 1)
                act.activation(sink_e[:, :], sink_in[:, :], ACT.Exp).then_inc(sink_exped, 1)

            def split_weights(c):
                a, w = W_AT[c], W_COLS[c]
                for k in range(KT):
                    act.wait_ge(w_loaded[k], 16 * (c + 1))
                    act.activation(w_hi[:, k, a:a + w], ws[:, k, 0:w], ACT.Copy, scale=nw[:, k:k + 1]).then_inc(w_high, 1)

            square_x(tile(0, 0))
            split_high(tile(0, 0), 0)
            split_high(tile(0, 0), 1)
            act.wait_ge(nw_loaded, 16)
            split_weights(0)
            square_x(tile(0, 1))
            split_high(tile(0, 1), 0)
            split_high(tile(0, 1), 1)
            split_weights(1)
            keys_values(tile(0, 0))
            act.wait_ge(k_normed, 1)
            act.wait_ge(v_copied, 1)
            act.dma_start(KW[P - 1:P, :, :], k_nat[s_rows, :]).then_inc(new_row, 16)
            act.dma_start(VW[P - 1:P, :, :], v_nat[s_rows, :]).then_inc(new_row, 16)
            act.dma_start(new_meta_k, k_nat[0:META, :]).then_inc(meta_stored, 16)
            act.dma_start(new_meta_v, v_nat[0:META, :]).then_inc(meta_stored, 16)
            keys_values(tile(0, 1))
            act.wait_ge(k_turned, 1)
            act.wait_ge(buffers_zeroed, 1)
            act.activation(KTS[:, :, :, 0:META], bank_t[:, :].rearrange("p (a b t) -> p a b t", a=KVH, b=2)[:, :, :, 0:META],
                           ACT.Copy).then_inc(k_placed, 1)
            square_q(tile(0, 0))
            square_x(tile(0, 2))
            split_weights(2)
            square_q(tile(0, 1))
            place_k(tile(0, 1))
            gate(tile(0, 0))
            split_high(tile(0, 2), 0)
            act.wait_ge(s_step, 3)
            act.activation(s_p[:, :], sc[0:64, 0, 0:P + META], ACT.Exp, bias=s_m[:, 0:1], scale=SCALE, accum_out=s_sum[:, :])
            act.activation(s_e[:, :], s_in[:, :], ACT.Exp).then_inc(s_exped, 1)
            split_high(tile(0, 2), 1)

            def iteration(t0, t1, t2, last, tail=True, ahead=True, more=True):
                if tail:
                    place_p(last, 3)
                if more:
                    square_x(t2)
                place_q(t0, 0)
                gate(t0)
                place_q(t0, 1)
                if ahead:
                    keys_values(t1)
                exps(t0, 0)
                if more:
                    split_high(t2, 0)
                if not ahead:
                    exps(t0, 1)
                    for j in range(2):
                        place_p(t0, j)
                        exps(t0, j + 2)
                    place_p(t0, 2)
                    sink_exp(t0)
                    return
                place_p(t0, 0)
                exps(t0, 1)
                square_q(t1)
                if more:
                    split_high(t2, 1)
                place_p(t0, 1)
                exps(t0, 2)
                place_p(t0, 2)
                exps(t0, 3)
                place_k(t1)
                sink_exp(t0)

            iteration(tile(0, 1), tile(0, 2), tile(0, 3), None, tail=False)
            with act.Fori(*LOOP) as it:
                for c in range(2):
                    iteration(tile(it, c), tile(it, c + 1), tile(it, c + 2), tile(it, c - 1))
            for n in range(LAST + 1, TILES):
                iteration(tile(0, n), tile(0, n + 1), tile(0, n + 2), tile(0, n - 1), ahead=n + 1 < TILES, more=n + 2 < TILES)
            place_p(tile(0, TILES - 1), 3)

        @block.vector
        def _(dve):
            dve.memset(X[0][:, :], 0.0).then_inc(x_zeroed, 1)

            def x_var(t):
                dve.wait_ge(x_squared, t.n + 1)
                wait(dve, rstd_done, t.n)
                dve.tensor_scalar(var[:, :], ss[:, :], 1.0 / D, EPS, ALU.mult, ALU.add).then_inc(var_done, 1)

            def x_scale(t):
                dve.wait_ge(rstd_done, t.n + 1)
                dve.tensor_scalar(X[t.slot][:, :], X[t.slot][:, :], rstd[:, 0:1], None, ALU.mult).then_inc(x_scaled, 1)

            def split_low(t, a):
                dve.wait_ge(h_high, 2 * t.n + a + 1)
                dve.tensor_tensor(half(h_lo[t.slot], a), x_bank(t, a)[:, :], half(h_hi[t.slot], a).bitcast(F32), ALU.subtract).then_inc(h_low, 1)

            def k_stats(t):
                dve.wait_ge(k_squared, t.n + 1)
                wait(dve, k_var, t.n)
                dve.tensor_reduce(kss[:, :], heads(sq_k[:, :]), AX.X, ALU.add).then_inc(k_summed, 1)
                dve.wait_ge(k_summed, t.n + 1)
                wait(dve, k_rstd, t.n)
                dve.tensor_scalar(kvar[:, :], kss[:, :], 1.0 / HD, EPS, ALU.mult, ALU.add).then_inc(k_var, 1)

            def k_norm(t):
                dve.wait_ge(k_rstd, t.n + 1)
                dve.wait_ge(v_copied, t.n + 1)
                wait(dve, k_low, t.n)
                if isinstance(t.n, int) and t.n == 1:
                    dve.wait_ge(new_row, 32)
                    dve.wait_ge(meta_stored, 2 * 16)
                for kv in range(KVH):
                    c = slice(kv * HD, (kv + 1) * HD)
                    ins = dve.scalar_tensor_tensor(k_nat[:, c], kv_bank(t)[:, c], krstd[:, kv:kv + 1], knw[:, :], ALU.mult, ALU.mult)
                ins.then_inc(k_normed, 1)
                dve.wait_ge(k_normed, t.n + 1)
                wait(dve, k_turned, t.n)
                twice = heads(k_nat[:, :]).unsqueeze(2).to_broadcast([P, KVH, 2, HD])
                dve.tensor_copy(KS[:, :, 0:2, :], twice).then_inc(k_high, 1)
                dve.wait_ge(k_high, t.n + 1)
                dve.tensor_tensor(KS[:, :, 2:4, :], twice, KS[:, :, 0:2, :].bitcast(F32), ALU.subtract).then_inc(k_low, 1)

            def q_stats(t):
                dve.wait_ge(q_squared, t.n + 1)
                wait(dve, q_var, t.n)
                dve.tensor_reduce(qss[:, :], heads(sq_q[:, :]), AX.X, ALU.add).then_inc(q_summed, 1)
                dve.wait_ge(q_summed, t.n + 1)
                wait(dve, q_rstd, t.n)
                dve.tensor_scalar(qvar[:, :], qss[:, :], 1.0 / HD, EPS, ALU.mult, ALU.add).then_inc(q_var, 1)

            def q_norm(t):
                dve.wait_ge(q_rstd, t.n + 1)
                wait(dve, q_low, t.n - 1)
                if isinstance(t.n, int) and t.n == 1:
                    dve.wait_ge(q_done, 1)
                dve.tensor_tensor(heads(q_nat[:, :]), heads(q_bank(t)[:, :]), qrstd[:, :].unsqueeze(2).to_broadcast([P, AH, HD]),
                                  ALU.mult).then_inc(q_normed, 1)

            def q_split(t):
                dve.wait_ge(q_done, t.n + 1)
                wait(dve, q_turned, 2 * (t.n - 1))
                dve.tensor_copy(QS[:, :, 0, :], heads(q_nat[:, :])).then_inc(q_high, 1)

            def gate_plus(t):
                dve.wait_ge(g_copied, t.n + 1)
                dve.tensor_scalar(g_exp[:, :], g_exp[:, :], 1.0, None, ALU.add).then_inc(g_plus, 1)

            def gate_recip(t, i):
                dve.wait_ge(g_plus, t.n + 1)
                wait(dve, g_ready, t.n)
                c = slice(P * i, P * i + P)
                dve.reciprocal(g_inv[:, c], g_exp[:, c]).then_inc(g_recip, 1)

            def gate_mul(t):
                dve.wait_ge(g_recip, 4 * t.n + 4)
                dve.tensor_tensor(G[t.slot][:, :], G[t.slot][:, :], g_inv[:, :], ALU.mult).then_inc(g_ready, 1)

            def maxima(t, j, mask):
                dve.wait_ge(scored, 4 * (t.n - 1) + j + 1)
                wait(dve, exped, 4 * (t.n - 1) + j - 1)
                wait(dve, sink_exped, t.n - 1)
                dve.sem_inc(max_begun, 1)
                for i in range(2):
                    h = 2 * j + i
                    ins = dve.tensor_tensor_reduce(SM[j % 2][:, i, :], sc[:, i, 0:KEYS], hidden[:, mask, :], -SCALE, neg_sink[:, h:h + 1],
                                                   ALU.add, ALU.min, accum_out=neg_m[:, h:h + 1])
                ins.then_inc(m_ready, 1)

            def sink_add(t):
                dve.wait_ge(m_ready, 4 * t.n)
                dve.tensor_tensor(sink_in[:, :], sink[:, :], neg_m[:, :], ALU.add).then_inc(sink_added, 1)

            def denominators(t):
                dve.wait_ge(sink_exped, t.n)
                dve.wait_ge(exped, 4 * t.n)
                dve.tensor_tensor(den[:, :], row_sum[:, :], sink_e[:, :], ALU.add).then_inc(sums_added, 1)
                dve.wait_ge(sums_added, t.n)
                dve.tensor_tensor(den[:, :], den[:, :], row_sum_meta[:, :], ALU.add).then_inc(den_done, 1)
                dve.wait_ge(den_done, t.n)
                wait(dve, o_normed, t.n)
                dve.reciprocal(rden[:, :], den[:, :]).then_inc(rden_done, 1)

            def o_norm(t):
                dve.wait_ge(o_ready, t.n)
                dve.wait_ge(rden_done, t.n)
                wait(dve, mix_done, t.n)
                dve.tensor_tensor(heads(o_nat[:, :]), heads(bank_o[:, :]), rden[:, :].unsqueeze(2).to_broadcast([P, AH, HD]),
                                  ALU.mult).then_inc(o_normed, 1)

            def place_v(t):
                dve.wait_ge(v_copied, t.n + 1)
                wait(dve, pv_done, 4 * (t.n - 1))
                if first_tile(t):
                    dve.tensor_copy(V_meta[:, :], v_nat[0:META, :])
                dve.tensor_copy(V[t.slot][:, :], v_nat[:, :]).then_inc(v_placed, 1)

            def split_weights(c):
                a, w = W_AT[c], W_COLS[c]
                for k in range(KT):
                    dve.wait_ge(w_high, KT * c + k + 1)
                    dve.scalar_tensor_tensor(w_lo[:, k, a:a + w], ws[:, k, 0:w], nw[:, k:k + 1], w_hi[:, k, a:a + w].bitcast(F32),
                                             ALU.mult, ALU.subtract).then_inc(w_ready, 1)

            x_var(tile(0, 0))
            x_scale(tile(0, 0))
            split_low(tile(0, 0), 0)
            split_low(tile(0, 0), 1)
            dve.wait_ge(nw_loaded, 16)
            split_weights(0)
            x_var(tile(0, 1))
            x_scale(tile(0, 1))
            split_low(tile(0, 1), 0)
            split_low(tile(0, 1), 1)
            split_weights(1)
            dve.wait_ge(sink_loaded, 5 * 16)
            dve.wait_ge(c_loaded, 16)
            k_stats(tile(0, 0))
            k_norm(tile(0, 0))
            place_v(tile(0, 0))
            dve.tensor_scalar(neg_sink[:, :], sink[:, :], -1.0, None, ALU.mult).then_inc(sink_negated, 1)
            dve.wait_ge(sink_negated, 1)
            k_stats(tile(0, 1))
            k_norm(tile(0, 1))
            q_stats(tile(0, 0))
            q_norm(tile(0, 0))
            split_weights(2)
            x_var(tile(0, 2))
            x_scale(tile(0, 2))
            q_stats(tile(0, 1))
            q_norm(tile(0, 1))
            dve.wait_ge(sk_turned, 1)
            dve.tensor_copy(KTW[:, :, 0:P].rearrange("p (a b) k -> p a b k", a=2), sc[:, :, :].rearrange("p a (b k) -> p a b k", k=P))
            dve.tensor_copy(KTW[:, :, P:P + META], bank_o[:, 0:NS * META].rearrange("p (b k) -> p b k", k=META)).then_inc(sk_placed, 1)
            dve.wait_ge(sq_turned, 1)
            dve.wait_ge(buffers_zeroed, 1)
            for kv in range(KVH):
                r = slice(kv * HD, (kv + 1) * HD)
                ins = dve.tensor_copy(QZ[r, :].rearrange("p (b c) -> p b c", c=72)[:, :, 4 * kv:4 * kv + 4],
                                      bank_t[r, :].rearrange("p (g t) -> p t g", g=4)[:, s_rows, :])
            ins.then_inc(sq_placed, 1)
            q_split(tile(0, 1))
            split_low(tile(0, 2), 0)
            dve.wait_ge(s_scored, 1)
            dve.tensor_reduce(s_neg[:, :], sc[0:64, 0, 0:P + META], AX.X, ALU.max, negate=True)
            dve.tensor_scalar(s_in[:, :], s_sink[:, :], -1.0, None, ALU.mult).then_inc(s_step, 1)
            dve.wait_ge(s_step, 1)
            dve.scalar_tensor_tensor(s_m[:, :], s_neg[:, :], SCALE, s_in[:, :], ALU.mult, ALU.min).then_inc(s_step, 1)
            dve.wait_ge(s_step, 2)
            dve.tensor_tensor(s_in[:, :], s_sink[:, :], s_m[:, :], ALU.add).then_inc(s_step, 1)
            gate_plus(tile(0, 0))
            gate_recip(tile(0, 0), 0)
            gate_recip(tile(0, 0), 1)
            split_low(tile(0, 2), 1)
            dve.wait_ge(s_exped, 1)
            dve.tensor_tensor(s_den[:, :], s_sum[:, :], s_e[:, :], ALU.add).then_inc(s_step, 1)
            dve.wait_ge(s_step, 4)
            dve.reciprocal(s_rden[:, :], s_den[:, :]).then_inc(s_step, 1)
            dve.wait_ge(sp_turned, 1)
            dve.tensor_copy(PZ[:, :].rearrange("p (b c) -> p b c", c=72)[:, :, 0:AH], pt[:, 0, 0:64].rearrange("p (b h) -> p b h", h=AH))
            dve.tensor_copy(PZM[:, :].rearrange("p (b c) -> p b c", c=72)[:, :, 0:AH],
                            pt[0:META, 0, 64:128].rearrange("p (b h) -> p b h", h=AH)).then_inc(sp_placed, 1)
            gate_recip(tile(0, 0), 2)
            gate_recip(tile(0, 0), 3)
            gate_mul(tile(0, 0))
            dve.wait_ge(s_pv, 1)
            dve.wait_ge(s_step, 5)
            dve.tensor_scalar(s_o[:, :], bank_o[0:64, 0:KVH * HD], s_rden[:, 0:1], None, ALU.mult).then_inc(o_normed, 1)

            def iteration(t0, t1, t2, last, mask, tail=True, ahead=True, more=True):
                if more:
                    x_var(t2)
                    x_scale(t2)
                if tail:
                    denominators(last)
                gate_plus(t0)
                if tail:
                    o_norm(last)
                place_v(t0)
                maxima(t0, 0, mask)
                if ahead:
                    k_stats(t1)
                    k_norm(t1)
                if more:
                    split_low(t2, 0)
                maxima(t0, 1, mask)
                gate_recip(t0, 0)
                gate_recip(t0, 1)
                if more:
                    split_low(t2, 1)
                maxima(t0, 2, mask)
                if ahead:
                    q_stats(t1)
                gate_recip(t0, 2)
                if ahead:
                    q_norm(t1)
                maxima(t0, 3, mask)
                sink_add(t0)
                gate_recip(t0, 3)
                if ahead:
                    q_split(t1)
                gate_mul(t0)

            iteration(tile(0, 1), tile(0, 2), tile(0, 3), None, 2, tail=False)
            dve.wait_ge(s_back, 32)
            dve.wait_ge(g_ready, 1)
            dve.tensor_tensor(s_nat[s_rows, :], s_nat[s_rows, :], G[0][s_rows, :], ALU.mult).then_inc(mix_done, 1)
            with dve.Fori(*LOOP) as it:
                for c in range(2):
                    iteration(tile(it, c), tile(it, c + 1), tile(it, c + 2), tile(it, c - 1), c)
            for n in range(LAST + 1, TILES):
                iteration(tile(0, n), tile(0, n + 1), tile(0, n + 2), tile(0, n - 1), n % 2, ahead=n + 1 < TILES, more=n + 2 < TILES)
            denominators(tile(0, TILES - 1))
            o_norm(tile(0, TILES - 1))

        @block.tensor
        def _(pe):
            def turn_x(t, a):
                pe.wait_ge(x_scaled, t.n + 1)
                for j in range(4):
                    ins = pe.transpose(x_bank(t, a)[:, j * P:(j + 1) * P], X[t.slot][:, (4 * a + j) * P:(4 * a + j + 1) * P], ident[:, :])
                ins.then_inc(xt, 1)

            def project(t, out, c, chunks, first=False):
                a, w = W_AT[c], W_COLS[c]
                for k in chunks:
                    if first:
                        pe.wait_ge(w_ready, KT * c + k + 1)
                        if (c, k) == (0, KT // 2):
                            pe.wait_ge(h_low, 2)
                    hi, lo = w_hi[:, k, a:a + w], w_lo[:, k, a:a + w]
                    pe.matmul(out[:, 0:w], h_hi[t.slot][:, k, :], hi, start=(k == 0), stop=False)
                    pe.matmul(out[:, 0:w], h_hi[t.slot][:, k, :], lo, start=False, stop=False)
                    ins = pe.matmul(out[:, 0:w], h_lo[t.slot][:, k, :], hi, start=False, stop=(k == KT - 1))
                return ins

            def turn_k(t):
                pe.wait_ge(k_low, t.n + 1)
                for kv in range(KVH):
                    for part in range(2):
                        at = (2 * kv + part) * P
                        ins = pe.transpose(bank_t[:, at:at + P],
                                           KS[:, kv, 2 * part:2 * part + 2, :].rearrange("p a d -> p (a d)").bitcast(F32), ident[:, :])
                ins.then_inc(k_turned, 1)

            def turn_q(t, a):
                pe.wait_ge(q_low, t.n) if isinstance(t.n, int) else pe.wait_ge(q_low, t.n)
                for i in range(4):
                    ins = pe.transpose(bank_t[:, i * P:(i + 1) * P],
                                       QS[:, 4 * a + i, :, :].rearrange("p a d -> p (a d)").bitcast(F32), ident[:, :])
                ins.then_inc(q_turned, 1)

            def scores(t, j):
                pe.wait_ge(q_placed, 2 * (t.n - 1) + j // 2 + 1)
                pe.wait_ge(k_placed, t.n + 1)
                wait(pe, m_ready, 4 * (t.n - 1) + j)
                for i in range(2):
                    h = 2 * j + i
                    kv = h // (AH // KVH)
                    pe.matmul(sc[:, i, 0:KEYS], QT[:, h, :], KTS[:, kv, 0, :], start=True, stop=False)
                    ins = pe.matmul(sc[:, i, 0:KEYS], QT[:, h, :], KTS[:, kv, 1, :], start=False, stop=True)
                ins.then_inc(scored, 1)

            def turn_p(t, j):
                pe.wait_ge(exped, 4 * (t.n - 1) + j + 1)
                wait(pe, p_placed, 4 * (t.n - 1) + j)
                for i in range(2):
                    pe.transpose(pt[:, i, 0:P], PRB[j % 2][:, i, 0:P], ident[:, :])
                    ins = pe.transpose(pt[:, i, P:2 * P], PRB[j % 2][:, i, P:2 * P], ident[:, :])
                if j == 3:
                    ins = pe.transpose(pt[:, 0, 2 * P:3 * P], PM[:, :, :].rearrange("p h k -> p (h k)"), ident[:, :])
                ins.then_inc(p_turned, 1)

            def values(t, j):
                pe.wait_ge(p_placed, 4 * (t.n - 1) + j + 1)
                if j == 0:
                    pe.wait_ge(v_placed, t.n + 1)
                    wait(pe, o_normed, t.n)
                for i in range(2):
                    h = 2 * j + i
                    kv = h // (AH // KVH)
                    c, out = slice(kv * HD, (kv + 1) * HD), bank_o[:, h * HD:(h + 1) * HD]
                    pe.matmul(out, PTS[:, i, 0:P], V[0][:, c], start=(h == 0), stop=False)
                    ins = pe.matmul(out, PTS[:, i, P:2 * P], V[1][:, c], start=False, stop=False)
                ins.then_inc(pv_done, 1)
                if j == 3:
                    pe.matmul(bank_o[:, :], PMT[:, :], VMD[:, :], start=False, stop=True).then_inc(o_ready, 1)

            pe.wait_ge(c_loaded, 16)
            t0, t1, t2 = tile(0, 0), tile(0, 1), tile(0, 2)
            turn_x(t0, 0)
            turn_x(t0, 1)
            pe.wait_ge(h_low, 1)
            project(t0, kv_bank(t0), 0, range(KT), True).then_inc(kv_proj, 1)
            turn_x(t1, 0)
            turn_x(t1, 1)
            pe.wait_ge(h_low, 4)
            project(t1, kv_bank(t1), 0, range(KT)).then_inc(kv_proj, 1)
            project(t0, q_bank(t0), 1, range(KT), True).then_inc(q_proj, 1)
            turn_k(t0)
            project(t1, q_bank(t1), 1, range(KT)).then_inc(q_proj, 1)
            pe.wait_ge(cache_loaded, 4 * 16)
            pe.wait_ge(new_row, 32)
            for b in range(NS):
                pe.transpose(sc[:, b // 4, (b % 4) * P:(b % 4 + 1) * P], KW[:, b, :], ident[:, :])
                ins = pe.transpose(bank_o[:, b * META:(b + 1) * META], KM[:, b, :], ident[0:META, 0:META])
            ins.then_inc(sk_turned, 1)
            pe.wait_ge(k_placed, 1)
            turn_k(t1)
            pe.wait_ge(k_normed, 1)
            pe.wait_ge(v_copied, 1)
            project(t0, kv_bank(t0), 2, range(KT), True).then_inc(g_proj, 1)
            pe.wait_ge(q_done, 1)
            pe.wait_ge(k_placed, 2)
            for g in range(4):
                ins = pe.transpose(bank_t[:, g * P:(g + 1) * P], o_nat[:, g * P:(g + 1) * P], ident[:, :])
            ins.then_inc(sq_turned, 1)
            pe.wait_ge(k_normed, 2)
            pe.wait_ge(v_copied, 2)
            project(t1, kv_bank(t1), 2, range(0, 4))
            pe.wait_ge(sk_placed, 1)
            pe.wait_ge(sq_placed, 1)
            turn_x(t2, 0)
            for b in range(NS):
                ins = pe.matmul(sc[0:64, 0, 0:P + META], QZ[:, 64 * b:64 * b + 64], KTW[:, b, :], start=(b == 0), stop=(b == NS - 1))
            ins.then_inc(s_scored, 1)
            project(t1, kv_bank(t1), 2, range(4, 8)).then_inc(g_proj, 1)
            pe.wait_ge(h_low, 5)
            turn_x(t2, 1)
            pe.wait_ge(s_exped, 1)
            pe.wait_ge(g_copied, 1)
            pe.transpose(pt[:, 0, 0:64], s_p[:, 0:P], ident[0:64, 0:64])
            pe.transpose(pt[0:META, 0, 64:128], s_p[:, P:P + META], ident[0:64, 0:64]).then_inc(sp_turned, 1)
            pe.wait_ge(h_low, 6)
            turn_q(t1, 0)
            pe.wait_ge(sp_placed, 1)
            for b in range(NS):
                c = slice(64 * b, 64 * b + 64)
                pe.matmul(bank_o[0:64, 0:KVH * HD], PZ[:, c], VW[:, b, :], start=(b == 0), stop=False)
                ins = pe.matmul(bank_o[0:64, 0:KVH * HD], PZM[:, c], VM[:, b, :], start=False, stop=(b == NS - 1))
            ins.then_inc(s_pv, 1)
            pe.wait_ge(v_meta_spread, AH * 16)

            def iteration(t0, t1, t2, last, tail=True, ahead=True, more=True):
                if ahead:
                    pe.wait_ge(q_normed, t0.n + 1)
                    pe.wait_ge(h_low, 2 * t1.n + 2)
                    project(t1, kv_bank(t1), 0, range(0, 4))
                if tail:
                    values(last, 3)
                pe.wait_ge(q_placed, 2 * t0.n - 1)
                turn_q(t0, 1)
                if ahead:
                    project(t1, kv_bank(t1), 0, range(4, 8)).then_inc(kv_proj, 1)
                scores(t0, 0)
                if not ahead:
                    for j in range(4):
                        if j < 3:
                            scores(t0, j + 1)
                        if j:
                            values(t0, j - 1)
                        turn_p(t0, j)
                    return
                pe.wait_ge(g_copied, t0.n + 1)
                project(t1, q_bank(t1), 1, range(0, 4))
                if more:
                    pe.wait_ge(q_placed, 2 * t0.n)
                    turn_x(t2, 0)
                turn_p(t0, 0)
                scores(t0, 1)
                project(t1, q_bank(t1), 1, range(4, 8)).then_inc(q_proj, 1)
                if more:
                    pe.wait_ge(h_low, 2 * t2.n + 1)
                    turn_x(t2, 1)
                values(t0, 0)
                turn_p(t0, 1)
                scores(t0, 2)
                pe.wait_ge(k_normed, t1.n + 1)
                pe.wait_ge(v_copied, t1.n + 1)
                project(t1, kv_bank(t1), 2, range(0, 4))
                values(t0, 1)
                turn_p(t0, 2)
                scores(t0, 3)
                if more:
                    pe.wait_ge(h_low, 2 * t2.n + 2)
                turn_k(t1)
                project(t1, kv_bank(t1), 2, range(4, 8)).then_inc(g_proj, 1)
                values(t0, 2)
                turn_p(t0, 3)
                pe.wait_ge(k_placed, t1.n + 1)
                turn_q(t1, 0)

            iteration(tile(0, 1), tile(0, 2), tile(0, 3), None, tail=False)
            with pe.Fori(*LOOP) as it:
                for c in range(2):
                    iteration(tile(it, c), tile(it, c + 1), tile(it, c + 2), tile(it, c - 1))
            for n in range(LAST + 1, TILES):
                iteration(tile(0, n), tile(0, n + 1), tile(0, n + 2), tile(0, n - 1), ahead=n + 1 < TILES, more=n + 2 < TILES)
            values(tile(0, TILES - 1), 3)


def output_pass(nc, x_prompt, x_sample, mixed, mixed_sample, w_out, consts, y_prompt, y_sample):
    with ExitStack() as ctx:
        def sb(name, shape, dt=F32):
            return ctx.enter_context(nc.sbuf_tensor("o_" + name, shape, dt))

        def bank(name):
            return ctx.enter_context(nc.psum_tensor("o_" + name, [P, 512], F32))

        def sem(name):
            return nc.alloc_semaphore(name="o_" + name)

        w_hi = sb("w_hi", [P, KT, D], F32R)
        w_lo = sb("w_lo", [P, KT, D], F32R)
        ws = sb("ws", [P, KT, HW])
        ident = sb("ident", [P, P])
        M = [sb(f"m{i}", [P, D]) for i in range(2)]
        X = [sb(f"x{i}", [P, D]) for i in range(2)]
        Y = [sb(f"y{i}", [P, D]) for i in range(2)]
        m_hi = [sb(f"m_hi{i}", [P, KT, P], F32R) for i in range(2)]
        m_lo = [sb(f"m_lo{i}", [P, KT, P], F32R) for i in range(2)]
        bank_t = [bank(f"bank_t{i}") for i in range(2)]
        bank_y = [[bank(f"bank_y{i}{a}") for a in range(2)] for i in range(2)]

        c_loaded, m_zeroed = sem("c_loaded"), sem("m_zeroed")
        w_loaded = [sem(f"w_loaded{i}") for i in range(KT)]
        w_high, w_ready = sem("w_high"), sem("w_ready")
        m_loaded, x_loaded, y_stored = ([sem(f"{name}{i}") for i in range(2)] for name in ("m_loaded", "x_loaded", "y_stored"))
        m_turned, m_high, m_low, multiplied, y_added = (sem(x) for x in ("m_turned", "m_high", "m_low", "multiplied", "y_added"))

        def part(buffer, a):
            return buffer[:, 4 * a:4 * a + 4, :].rearrange("p k t -> p (k t)")

        def cols(a):
            return slice(a * HW, (a + 1) * HW)

        block = ctx.enter_context(nc.Block())

        @block.sync
        def _(sp):
            def load_mixed(t):
                wait(sp, m_turned, 2 * (t.n - 1))
                sp.dma_start(M[t.slot][:, :], rows_of(mixed, t)).then_inc(m_loaded[t.slot], 16)

            def load_x(t):
                wait(sp, y_added, 2 * (t.n - 1))
                sp.dma_start(X[t.slot][:, :], rows_of(x_prompt, t)).then_inc(x_loaded[t.slot], 16)

            def store_y(t):
                sp.wait_ge(y_added, 2 * t.n + 2)
                sp.dma_start(rows_of(y_prompt, t), Y[t.slot][:, :]).then_inc(y_stored[t.slot], 16)

            sp.dma_start(ident[:, :], consts[:, 0:P]).then_inc(c_loaded, 16)
            sp.wait_ge(m_zeroed, 1)
            sp.dma_start(M[0][0:NS, :], mixed_sample).then_inc(m_loaded[0], 16)
            for a in range(2):
                for k in range(KT):
                    j = KT * a + k
                    wait(sp, w_ready, j + 1 - KT)
                    sp.dma_start(ws[:, k, :], w_out[k * P:(k + 1) * P, cols(a)]).then_inc(w_loaded[k], 16)
                if a == 0:
                    load_mixed(tile(0, 1))
            sp.dma_start(X[0][0:NS, :], x_sample).then_inc(x_loaded[0], 16)
            load_x(tile(0, 1))
            load_mixed(tile(0, 2))
            sp.wait_ge(y_added, 2)
            sp.dma_start(y_sample, Y[0][0:NS, :]).then_inc(y_stored[0], 16)
            load_x(tile(0, 2))
            load_mixed(tile(0, 3))
            store_y(tile(0, 1))
            load_x(tile(0, 3))
            with sp.Fori(1, TILES // 2 - 1) as it:
                for c in range(2):
                    load_mixed(tile(it, c + 2))
                    store_y(tile(it, c))
                    load_x(tile(it, c + 2))
            for n in range(TILES - 3, TILES):
                if n + 2 < TILES:
                    load_mixed(tile(0, n + 2))
                store_y(tile(0, n))
                if n + 2 < TILES:
                    load_x(tile(0, n + 2))
            for i in range(2):
                sp.wait_ge(y_stored[i], 16 * ((TILES + 1 - i) // 2))

        @block.scalar
        def _(act):
            def split_high(t, a):
                act.wait_ge(m_turned, 2 * t.n + a + 1)
                wait(act, multiplied, 2 * (t.n - 1))
                act.activation(part(m_hi[t.slot], a), bank_t[a][:, :], ACT.Copy).then_inc(m_high, 1)

            def split_weights(a):
                for k in range(KT):
                    act.wait_ge(w_loaded[k], 16 * (a + 1))
                    act.activation(w_hi[:, k, cols(a)], ws[:, k, :], ACT.Copy).then_inc(w_high, 1)

            for a in range(2):
                split_high(tile(0, 0), a)
            split_weights(0)
            for a in range(2):
                split_high(tile(0, 1), a)
            split_weights(1)
            with act.Fori(1, TILES // 2) as it:
                for c in range(2):
                    for a in range(2):
                        split_high(tile(it, c), a)
            for a in range(2):
                split_high(tile(0, TILES - 1), a)

        @block.vector
        def _(dve):
            dve.memset(M[0][:, :], 0.0).then_inc(m_zeroed, 1)

            def split_low(t, a):
                dve.wait_ge(m_high, 2 * t.n + a + 1)
                dve.tensor_tensor(part(m_lo[t.slot], a), bank_t[a][:, :], part(m_hi[t.slot], a).bitcast(F32),
                                  ALU.subtract).then_inc(m_low, 1)

            def split_weights(a):
                for k in range(KT):
                    dve.wait_ge(w_high, KT * a + k + 1)
                    dve.tensor_tensor(w_lo[:, k, cols(a)], ws[:, k, :], w_hi[:, k, cols(a)].bitcast(F32),
                                      ALU.subtract).then_inc(w_ready, 1)

            def add_x(t, a, rows=P):
                dve.wait_ge(multiplied, 2 * t.n + a + 1)
                dve.wait_ge(x_loaded[t.slot], 16 * (t.half + 1))
                wait(dve, y_stored[t.slot], 16 * t.half)
                dve.tensor_tensor(Y[t.slot][0:rows, cols(a)], bank_y[t.slot][a][0:rows, :], X[t.slot][0:rows, cols(a)],
                                  ALU.add).then_inc(y_added, 1)

            for a in range(2):
                split_low(tile(0, 0), a)
            split_weights(0)
            split_low(tile(0, 1), 0)
            split_low(tile(0, 1), 1)
            split_weights(1)
            add_x(tile(0, 0), 0, NS)
            add_x(tile(0, 0), 1, NS)
            split_low(tile(0, 2), 0)
            add_x(tile(0, 1), 0)
            split_low(tile(0, 2), 1)
            add_x(tile(0, 1), 1)
            with dve.Fori(1, TILES // 2) as it:
                for c in range(2):
                    for a in range(2):
                        split_low(tile(it, c + 1), a)
                        add_x(tile(it, c), a)
            for a in range(2):
                add_x(tile(0, TILES - 1), a)

        @block.tensor
        def _(pe):
            def turn(t, a):
                pe.wait_ge(m_loaded[t.slot], 16 * (t.half + 1))
                wait(pe, m_low, 2 * t.n + a - 1)
                for j in range(4):
                    c = slice((4 * a + j) * P, (4 * a + j + 1) * P)
                    ins = pe.transpose(bank_t[a][:, j * P:(j + 1) * P], M[t.slot][:, c], ident[:, :])
                ins.then_inc(m_turned, 1)

            def multiply(t, a, chunks=range(KT), first=False):
                pe.wait_ge(m_low, 2 * t.n + (1 if first and a == 0 else 2))
                wait(pe, y_added, 2 * (t.n - 2) + a + 1)
                out = bank_y[t.slot][a][:, :]
                for k in chunks:
                    if first:
                        pe.wait_ge(w_ready, KT * a + k + 1)
                        if (a, k) == (0, KT // 2):
                            pe.wait_ge(m_low, 2)
                    hi, lo = m_hi[t.slot][:, k, :], m_lo[t.slot][:, k, :]
                    pe.matmul(out, hi, w_hi[:, k, cols(a)], start=(k == 0), stop=False)
                    pe.matmul(out, hi, w_lo[:, k, cols(a)], start=False, stop=False)
                    ins = pe.matmul(out, lo, w_hi[:, k, cols(a)], start=False, stop=(k == KT - 1))
                return ins

            def iteration(t, ahead):
                for a in range(2):
                    if ahead:
                        turn(ahead, a)
                    multiply(t, a).then_inc(multiplied, 1)

            pe.wait_ge(c_loaded, 16)
            turn(tile(0, 0), 0)
            turn(tile(0, 0), 1)
            multiply(tile(0, 0), 0, first=True).then_inc(multiplied, 1)
            turn(tile(0, 1), 0)
            turn(tile(0, 1), 1)
            multiply(tile(0, 1), 0)
            multiply(tile(0, 0), 1, first=True).then_inc(multiplied, 1)
            turn(tile(0, 2), 0)
            multiply(tile(0, 1), 1, range(0, 4)).then_inc(multiplied, 1)
            turn(tile(0, 2), 1)
            multiply(tile(0, 1), 1, range(4, KT)).then_inc(multiplied, 1)
            with pe.Fori(1, TILES // 2) as it:
                for c in range(2):
                    iteration(tile(it, c), tile(it, c + 1))
            iteration(tile(0, TILES - 1), None)


def layer(nc, a):
    def pick(*names):
        return {name: a[name] for name in names}

    for name, shape in (("mixed", (SEQ, D)), ("mixed_sample", (NS, D)), ("sample_o", (NS * AH, KVH * HD))):
        a[name] = nc.dram_tensor(name, shape, F32, kind="Internal").ap()
    rows = ("x_prompt", "x_sample", "meta_tokens", "w_in", "norm_w", "consts", "mixed", "mixed_sample")
    with nc.cleanup_on_exit():
        hgrn_pass(nc, **pick(*rows, "lb_logits", "hg_norm_w", "state", "new_state", "new_state_sample"))
    with nc.cleanup_on_exit():
        attention_pass(nc, **pick(*rows, "q_norm_w", "k_norm_w", "sinks", "sinks_rows", "masks", "win_k", "win_v", "meta_k", "meta_v",
                                  "sample_o", "new_win_k", "new_win_v", "new_meta_k", "new_meta_v",
                                  "new_win_k_sample", "new_win_v_sample"))
    output_pass(nc, **pick("x_prompt", "x_sample", "mixed", "mixed_sample", "w_out", "consts", "y_prompt", "y_sample"))


def shape_constants():
    s, t = np.arange(P)[:, None], np.arange(P)[None]
    s32, t32 = s % 32, t[:, :32]
    near = [s32 == t32] + [(s32 // (2 * b) == t32 // (2 * b)) & (s32 % (2 * b) < b) & (t32 % (2 * b) >= b) for b in PAIRS]
    consts = np.concatenate([np.eye(P)] + near, axis=1).astype(np.float32)
    q, k = s, t
    hidden = np.full((P, P), -1e30)
    current, previous, meta = np.where(k <= q, 0.0, hidden), np.where(k > q, 0.0, hidden), np.zeros((P, META))
    masks = np.stack([np.concatenate(m, axis=1) for m in
                      ((meta, current, previous), (meta, previous, current), (meta, hidden, current))], axis=1)
    return consts, masks.astype(np.float32)


def kernel(**inputs):
    import concourse.bacc as bacc
    from concourse.bass_utils import run_bass_kernel_spmd

    consts, masks = shape_constants()
    i = {name: np.asarray(value) for name, value in inputs.items()}

    def by_partition(vector):
        return vector.reshape(-1, P).T

    arrays = dict(
        x_prompt=i["x_prompt"][0], x_sample=i["x_sample"][:, 0], meta_tokens=i["meta_tokens"],
        w_in=i["w_in"][0], w_out=i["w_out"][0],
        norm_w=by_partition(i["norm_w"][0]), lb_logits=by_partition(i["hg_lb_logits"][0]),
        hg_norm_w=i["hg_norm_w"], q_norm_w=i["q_norm_w"], k_norm_w=i["k_norm_w"],
        sinks=i["attn_sinks"], sinks_rows=np.tile(i["attn_sinks"][0], NS)[:, None],
        state=i["state_hgrn"][:, 0],
        win_k=i["cache_win_k"].reshape(NS, P, KVH * HD), win_v=i["cache_win_v"].reshape(NS, P, KVH * HD),
        meta_k=i["cache_meta_k"].reshape(NS, META, KVH * HD), meta_v=i["cache_meta_v"].reshape(NS, META, KVH * HD),
        consts=consts, masks=masks)
    outputs = dict(
        y_prompt=(SEQ, D), y_sample=(NS, D), new_win_k=(P, KVH * HD), new_win_v=(P, KVH * HD),
        new_meta_k=(META, KVH * HD), new_meta_v=(META, KVH * HD), new_state=(HH, P, P),
        new_win_k_sample=(NS, P, KVH * HD), new_win_v_sample=(NS, P, KVH * HD), new_state_sample=(NS, HH, P, P))

    nc = bacc.Bacc("TRN2", target_bir_lowering=False, num_devices=1)
    arrays = {name: np.ascontiguousarray(value) for name, value in arrays.items()}
    dram = {name: nc.dram_tensor(name, value.shape, mybir.dt.from_np(value.dtype), kind="ExternalInput").ap()
            for name, value in arrays.items()}
    for name, shape in outputs.items():
        dram[name] = nc.dram_tensor(name, shape, F32, kind="ExternalOutput").ap()
    layer(nc, dram)
    got = run_bass_kernel_spmd(nc, [arrays], core_ids=[0]).results[0]
    return (got["y_prompt"].reshape(1, SEQ, D), got["y_sample"].reshape(NS, 1, D),
            got["new_win_k"].reshape(1, 1, P, KVH, HD), got["new_win_v"].reshape(1, 1, P, KVH, HD),
            got["new_meta_k"].reshape(1, 1, META, KVH, HD), got["new_meta_v"].reshape(1, 1, META, KVH, HD),
            got["new_state"].reshape(1, 1, HH, P, P),
            got["new_win_k_sample"].reshape(NS, 1, P, KVH, HD), got["new_win_v_sample"].reshape(NS, 1, P, KVH, HD),
            got["new_state_sample"].reshape(NS, 1, HH, P, P))
```
